# Optimizing a Trainium2 kernel written in Bass

```python
import math, functools
import jax, jax.numpy as jnp
from jax import lax
import numpy as np

D_MODEL = 1024
BATCH = 1
SEQ = 512
DEPTH = 2

GRID_W = 64
CTX_LEN = 256
HEAD_DIM = 64
RET_HEADS = 4
HG_HEADS = 4
ATT_Q_HEADS = 4
ATT_KV_HEADS = 2
GDN_HEADS = 4
BRANCH_W = 4 * HEAD_DIM
N_BRANCHES = 4
RET_CHUNK = 128
HG_CHUNK = 64
GDN_CHUNK = 64
ATT_BLOCK = 128
ROPE_THETA = 10000.0
ROPE_AXIS_DIM = HEAD_DIM // 2
CONV_W = 3
N_EXPERTS = 16
EXPERT_FF = 1024
CAPACITY_FACTOR = 2
EPS = 1e-6
F32 = jnp.float32

IN_SPLITS = (
    ('ret_q', RET_HEADS * HEAD_DIM), ('ret_k', RET_HEADS * HEAD_DIM), ('ret_v', RET_HEADS * HEAD_DIM),
    ('ret_g', RET_HEADS * HEAD_DIM),
    ('hg_q', HG_HEADS * HEAD_DIM), ('hg_f_fwd', HG_HEADS * HEAD_DIM), ('hg_f_bwd', HG_HEADS * HEAD_DIM),
    ('hg_i', HG_HEADS * HEAD_DIM), ('hg_g', HG_HEADS * HEAD_DIM),
    ('at_q', ATT_Q_HEADS * HEAD_DIM), ('at_k', ATT_KV_HEADS * HEAD_DIM), ('at_v', ATT_KV_HEADS * HEAD_DIM),
    ('gd_q', GDN_HEADS * HEAD_DIM), ('gd_k', GDN_HEADS * HEAD_DIM), ('gd_v', GDN_HEADS * HEAD_DIM),
    ('gd_a_fwd', GDN_HEADS), ('gd_a_bwd', GDN_HEADS), ('gd_b_fwd', GDN_HEADS), ('gd_b_bwd', GDN_HEADS),
    ('gd_g', GDN_HEADS * HEAD_DIM),
)
D_IN = sum(width for _, width in IN_SPLITS)

kernel_name = 'hybrid_quad_mixer_ec_moe'

def rmsnorm(x, g):
    x32 = x.astype(F32)
    y = x32 * lax.rsqrt(jnp.mean(x32 * x32, axis=-1, keepdims=True) + EPS)
    return (y * g.astype(F32)).astype(x.dtype)

def l2norm(x):
    return x * lax.rsqrt(jnp.sum(x * x, axis=-1, keepdims=True) + EPS)

def modulate(h, shift, scale):
    return h * (1 + scale) + shift

def to_heads(z, n_heads):
    b, l, _ = z.shape
    return z.reshape(b, l, n_heads, -1).transpose(0, 2, 1, 3).astype(F32)

def head_norm_gate(o, g, gate):
    b, h, l, d = o.shape
    o = rmsnorm(o.transpose(0, 2, 1, 3), g).reshape(b, l, h * d)
    return o.astype(gate.dtype) * jax.nn.silu(gate)

def split_cols(z):
    out, start = {}, 0
    for name, width in IN_SPLITS:
        out[name] = z[..., start:start + width]
        start += width
    return out

def axial_rope_tables(n_tokens):
    rows = n_tokens // GRID_W
    row = jnp.repeat(jnp.arange(rows, dtype=F32), GRID_W)
    col = jnp.tile(jnp.arange(GRID_W, dtype=F32), rows)
    inv_freq = ROPE_THETA ** (-jnp.arange(0, ROPE_AXIS_DIM, 2, dtype=F32) / ROPE_AXIS_DIM)
    ang = jnp.stack([row[:, None] * inv_freq, col[:, None] * inv_freq], axis=1)
    return jnp.cos(ang), jnp.sin(ang)

def apply_rope(x, cos, sin):
    half = ROPE_AXIS_DIM // 2
    xr = x.astype(F32).reshape(x.shape[:-1] + (2, 2, half))
    x1, x2 = xr[..., 0, :], xr[..., 1, :]
    c, s = cos[None, :, None], sin[None, :, None]
    out = jnp.stack([x1 * c - x2 * s, x2 * c + x1 * s], axis=-2)
    return out.reshape(x.shape).astype(x.dtype)

def dwconv_centred(x, w):
    ch = x.shape[-1]
    return lax.conv_general_dilated(x, w[:, None, :].astype(x.dtype), window_strides=(1,),
                                    padding=[(CONV_W // 2, CONV_W // 2)],
                                    dimension_numbers=('NWC', 'WIO', 'NWC'), feature_group_count=ch)

def chunk_states(chunk_decay, ds, s0):
    chunk_decay = jnp.broadcast_to(chunk_decay, ds.shape[:4] + (1,))

    def step(s, inp):
        a, d = inp
        return a * s + d, s

    s_final, s_start = lax.scan(step, s0, (jnp.moveaxis(chunk_decay, 2, 0), jnp.moveaxis(ds, 2, 0)))
    return jnp.moveaxis(s_start, 0, 2), s_final

def retention_chunked(q, k, v, s0, need_out, log_gamma):
    b, h, l, dk = q.shape
    dv = v.shape[-1]
    n = l // RET_CHUNK
    q = q.reshape(b, h, n, RET_CHUNK, dk)
    k = k.reshape(b, h, n, RET_CHUNK, dk)
    v = v.reshape(b, h, n, RET_CHUNK, dv)
    pos = jnp.arange(RET_CHUNK, dtype=F32)
    lg = log_gamma.astype(F32)[:, None]
    k_dec = jnp.exp(lg * (RET_CHUNK - 1 - pos))[None, :, None, :, None]
    ds = jnp.einsum('bhnsd,bhnsv->bhndv', k * k_dec, v)
    s_start, s_final = chunk_states(jnp.exp(lg * RET_CHUNK)[None, :, None, :, None], ds, s0)
    if not need_out:
        return None, s_final
    rel = pos[:, None] - pos[None, :]
    dmat = jnp.where(rel >= 0, jnp.exp(lg[:, :, None] * jnp.maximum(rel, 0.0)), 0.0)
    scores = jnp.einsum('bhntd,bhnsd->bhnts', q, k) * dmat[None, :, None]
    q_dec = jnp.exp(lg * (pos + 1))[None, :, None, :, None]
    o = jnp.einsum('bhnts,bhnsv->bhntv', scores, v) + jnp.einsum('bhntd,bhndv->bhntv', q * q_dec, s_start)
    return o.reshape(b, h, l, dv), s_final

def gla_chunked(q, k, v, log_f, s0, need_out):
    b, h, l, dk = q.shape
    dv = v.shape[-1]
    n = l // HG_CHUNK
    q, k, log_f = (t.reshape(b, h, n, HG_CHUNK, dk) for t in (q, k, log_f))
    v = v.reshape(b, h, n, HG_CHUNK, dv)
    cum = jnp.cumsum(log_f, axis=3)
    last = cum[:, :, :, -1:, :]
    ds = jnp.einsum('bhnsd,bhnsv->bhndv', k * jnp.exp(last - cum), v)
    s_start, s_final = chunk_states(jnp.swapaxes(jnp.exp(last), 3, 4), ds, s0)
    if not need_out:
        return None, s_final
    pos = jnp.arange(HG_CHUNK)
    causal = (pos[:, None] >= pos[None, :])[:, :, None]

    def intra(blk):
        qc, kc, vc, cc = blk
        diff = cc[:, :, :, None, :] - cc[:, :, None, :, :]
        decay = jnp.where(causal, jnp.exp(jnp.where(causal, diff, 0.0)), 0.0)
        scores = jnp.einsum('bhtd,bhsd,bhtsd->bhts', qc, kc, decay)
        return jnp.einsum('bhts,bhsv->bhtv', scores, vc)

    o_intra = jnp.moveaxis(lax.map(intra, tuple(jnp.moveaxis(t, 2, 0) for t in (q, k, v, cum))), 0, 2)
    o = o_intra + jnp.einsum('bhntd,bhndv->bhntv', q * jnp.exp(cum), s_start)
    return o.reshape(b, h, l, dv), s_final

def gdn_chunked(q, k, v, g, beta, s0, need_out):
    b, h, l, dk = q.shape
    dv = v.shape[-1]
    n = l // GDN_CHUNK
    q = q.reshape(b, h, n, GDN_CHUNK, dk)
    k = k.reshape(b, h, n, GDN_CHUNK, dk)
    v = v.reshape(b, h, n, GDN_CHUNK, dv)
    g = g.reshape(b, h, n, GDN_CHUNK)
    beta = beta.reshape(b, h, n, GDN_CHUNK)
    cg = jnp.cumsum(g, axis=-1)
    diff = cg[..., :, None] - cg[..., None, :]
    pos = jnp.arange(GDN_CHUNK)
    strict = pos[:, None] > pos[None, :]
    causal = pos[:, None] >= pos[None, :]
    kk = jnp.einsum('bhntd,bhnsd->bhnts', k, k)
    a_mat = jnp.where(strict, beta[..., None] * kk * jnp.exp(jnp.where(strict, diff, 0.0)), 0.0)
    rhs = jnp.concatenate([v * beta[..., None], k * (beta * jnp.exp(cg))[..., None]], axis=-1)
    sol = lax.linalg.triangular_solve(a_mat, rhs, left_side=True, lower=True, unit_diagonal=True)
    u, w = sol[..., :dv], sol[..., dv:]
    g_last = cg[..., -1:]
    k_tail = k * jnp.exp(g_last - cg)[..., None]
    chunk_decay = jnp.exp(g_last)[..., None]

    def step(s, inp):
        u_c, w_c, k_c, a_c = inp
        delta = u_c - w_c @ s
        return a_c * s + jnp.einsum('bhsd,bhsv->bhdv', k_c, delta), s

    s_final, s_start = lax.scan(step, s0, tuple(jnp.moveaxis(t, 2, 0) for t in (u, w, k_tail, chunk_decay)))
    if not need_out:
        return None, s_final
    s_start = jnp.moveaxis(s_start, 0, 2)
    delta = u - jnp.einsum('bhntd,bhndv->bhntv', w, s_start)
    pmat = jnp.where(causal, jnp.einsum('bhntd,bhnsd->bhnts', q, k) * jnp.exp(jnp.where(causal, diff, 0.0)), 0.0)
    o = (jnp.einsum('bhntd,bhndv->bhntv', q * jnp.exp(cg)[..., None], s_start)
         + jnp.einsum('bhnts,bhnsv->bhntv', pmat, delta))
    return o.reshape(b, h, l, dv), s_final

def bidirectional(fn_f, fn_b, ctx_f, lat_f, ctx_b, lat_b, s0, need_ctx):
    flip = lambda a: jnp.flip(a, axis=2)
    oc_f, sc_f = fn_f(*ctx_f, s0, need_ctx)
    ol_f, _ = fn_f(*lat_f, sc_f, True)
    oc_b, sc_b = fn_b(*[flip(a) for a in ctx_b], s0, need_ctx)
    ol_b, _ = fn_b(*[flip(a) for a in lat_b], sc_b, True)
    o_lat = ol_f + flip(ol_b)
    o_ctx = oc_f + flip(oc_b) if need_ctx else None
    return o_ctx, o_lat

def retention_mixer(pc, pl, cos, sin, norm_g, need_ctx):
    def prep(p, rope):
        b, l, _ = p['ret_q'].shape
        q = p['ret_q'].reshape(b, l, RET_HEADS, HEAD_DIM)
        k = p['ret_k'].reshape(b, l, RET_HEADS, HEAD_DIM) * (HEAD_DIM ** -0.5)
        if rope:
            q, k = apply_rope(q, cos, sin), apply_rope(k, cos, sin)
        return (q.transpose(0, 2, 1, 3).astype(F32), k.transpose(0, 2, 1, 3).astype(F32),
                to_heads(p['ret_v'], RET_HEADS))

    log_gamma = jnp.log1p(-jnp.exp2(-5.0 - jnp.arange(RET_HEADS, dtype=F32)))
    fn_f = functools.partial(retention_chunked, log_gamma=log_gamma)
    fn_b = functools.partial(retention_chunked, log_gamma=log_gamma[::-1])
    ctx_args, lat_args = prep(pc, False), prep(pl, True)
    s0 = jnp.zeros((pl['ret_q'].shape[0], RET_HEADS, HEAD_DIM, HEAD_DIM), F32)
    o_c, o_l = bidirectional(fn_f, fn_b, ctx_args, lat_args, ctx_args, lat_args, s0, need_ctx)
    y_lat = head_norm_gate(o_l, norm_g, pl['ret_g'])
    y_ctx = head_norm_gate(o_c, norm_g, pc['ret_g']) if need_ctx else None
    return y_ctx, y_lat

def hgrn2_mixer(pc, pl, lb_f, lb_b, norm_g, need_ctx):
    def forget(z, lb):
        z = z.astype(F32)
        f = lb + (1.0 - lb) * jax.nn.sigmoid(z)
        log_f = jnp.log(f)
        k = (1.0 - lb) * jax.nn.sigmoid(-z)
        return to_heads(k, HG_HEADS), to_heads(log_f, HG_HEADS)

    def prep(p):
        q = to_heads(jax.nn.silu(p['hg_q']), HG_HEADS)
        i = to_heads(p['hg_i'], HG_HEADS)
        k_f, lf_f = forget(p['hg_f_fwd'], lb_f)
        k_b, lf_b = forget(p['hg_f_bwd'], lb_b)
        return (q, k_f, i, lf_f), (q, k_b, i, lf_b)

    ctx_f, ctx_b = prep(pc)
    lat_f, lat_b = prep(pl)
    s0 = jnp.zeros((pl['hg_q'].shape[0], HG_HEADS, HEAD_DIM, HEAD_DIM), F32)
    o_c, o_l = bidirectional(gla_chunked, gla_chunked, ctx_f, lat_f, ctx_b, lat_b, s0, need_ctx)
    y_lat = head_norm_gate(o_l, norm_g, pl['hg_g'])
    y_ctx = head_norm_gate(o_c, norm_g, pc['hg_g']) if need_ctx else None
    return y_ctx, y_lat

def sdpa_block(qb, k, v):
    s = jnp.einsum('bhgtd,bhsd->bhgts', qb, k).astype(F32) * (HEAD_DIM ** -0.5)
    p = jax.nn.softmax(s, axis=-1).astype(v.dtype)
    return jnp.einsum('bhgts,bhsd->bhgtd', p, v)

def gqa_mixer(pc, pl, cos, sin, q_g, k_g, need_ctx):
    groups = ATT_Q_HEADS // ATT_KV_HEADS

    def prep_q(p, rope):
        b, l, _ = p['at_q'].shape
        q = rmsnorm(p['at_q'].reshape(b, l, ATT_Q_HEADS, HEAD_DIM), q_g)
        if rope:
            q = apply_rope(q, cos, sin)
        return q.reshape(b, l, ATT_KV_HEADS, groups, HEAD_DIM)

    def prep_kv(p, rope):
        b, l, _ = p['at_k'].shape
        k = rmsnorm(p['at_k'].reshape(b, l, ATT_KV_HEADS, HEAD_DIM), k_g)
        if rope:
            k = apply_rope(k, cos, sin)
        return k, p['at_v'].reshape(b, l, ATT_KV_HEADS, HEAD_DIM)

    kc, vc = prep_kv(pc, False)
    kl, vl = prep_kv(pl, True)
    ql = prep_q(pl, True)
    b, l = ql.shape[:2]
    k_all = jnp.concatenate([kc, kl], axis=1).transpose(0, 2, 1, 3)
    v_all = jnp.concatenate([vc, vl], axis=1).transpose(0, 2, 1, 3)
    n_blocks = l // ATT_BLOCK
    q_blocks = ql.reshape(b, n_blocks, ATT_BLOCK, ATT_KV_HEADS, groups, HEAD_DIM).transpose(1, 0, 3, 4, 2, 5)
    o = lax.map(lambda qb: sdpa_block(qb, k_all, v_all), q_blocks)
    y_lat = o.transpose(1, 0, 4, 2, 3, 5).reshape(b, l, ATT_Q_HEADS * HEAD_DIM)
    y_ctx = None
    if need_ctx:
        qc = prep_q(pc, False)
        lc = qc.shape[1]
        o_c = sdpa_block(qc.transpose(0, 2, 3, 1, 4), kc.transpose(0, 2, 1, 3), vc.transpose(0, 2, 1, 3))
        y_ctx = o_c.transpose(0, 3, 1, 2, 4).reshape(b, lc, ATT_Q_HEADS * HEAD_DIM)
    return y_ctx, y_lat

def gdn_mixer(pc, pl, conv_w, a_log, dt_bias, norm_g, need_ctx):
    def prep(p):
        qkv = jnp.concatenate([p['gd_q'], p['gd_k'], p['gd_v']], axis=-1)
        qkv = jax.nn.silu(dwconv_centred(qkv, conv_w))
        q, k, v = jnp.split(qkv, 3, axis=-1)
        q = l2norm(to_heads(q, GDN_HEADS)) * (HEAD_DIM ** -0.5)
        k = l2norm(to_heads(k, GDN_HEADS))
        v = to_heads(v, GDN_HEADS)

        def gates(a, bb, d):
            g = -jnp.exp(a_log[d].astype(F32)) * jax.nn.softplus(a.astype(F32) + dt_bias[d].astype(F32))
            beta = jax.nn.sigmoid(bb.astype(F32))
            return jnp.swapaxes(g, 1, 2), jnp.swapaxes(beta, 1, 2)

        g_f, beta_f = gates(p['gd_a_fwd'], p['gd_b_fwd'], 0)
        g_b, beta_b = gates(p['gd_a_bwd'], p['gd_b_bwd'], 1)
        return (q, k, v, g_f, beta_f), (q, k, v, g_b, beta_b)

    ctx_f, ctx_b = prep(pc)
    lat_f, lat_b = prep(pl)
    s0 = jnp.zeros((pl['gd_q'].shape[0], GDN_HEADS, HEAD_DIM, HEAD_DIM), F32)
    o_c, o_l = bidirectional(gdn_chunked, gdn_chunked, ctx_f, lat_f, ctx_b, lat_b, s0, need_ctx)
    y_lat = head_norm_gate(o_l, norm_g, pl['gd_g'])
    y_ctx = head_norm_gate(o_c, norm_g, pc['gd_g']) if need_ctx else None
    return y_ctx, y_lat

def merge_branches(h, ys, w_branch, w_merge, w_out):
    m = jax.nn.sigmoid(h @ w_merge[0]) * (ys[0] @ w_branch[0])
    for n in range(1, N_BRANCHES):
        m = m + jax.nn.sigmoid(h @ w_merge[n]) * (ys[n] @ w_branch[n])
    return m @ w_out

def token_mixer(h_ctx, h_lat, p, lb_f, lb_b, cos, sin, need_ctx):
    pc = split_cols(h_ctx @ p['w_in'])
    pl = split_cols(h_lat @ p['w_in'])
    ya_c, ya_l = retention_mixer(pc, pl, cos, sin, p['ret_norm_g'], need_ctx)
    yb_c, yb_l = hgrn2_mixer(pc, pl, lb_f, lb_b, p['hg_norm_g'], need_ctx)
    yc_c, yc_l = gqa_mixer(pc, pl, cos, sin, p['at_q_norm_g'], p['at_k_norm_g'], need_ctx)
    yd_c, yd_l = gdn_mixer(pc, pl, p['gd_conv_w'], p['gd_a_log'], p['gd_dt_bias'], p['gd_norm_g'], need_ctx)
    y_lat = merge_branches(h_lat, (ya_l, yb_l, yc_l, yd_l), p['w_branch'], p['w_merge'], p['w_out'])
    y_ctx = None
    if need_ctx:
        y_ctx = merge_branches(h_ctx, (ya_c, yb_c, yc_c, yd_c), p['w_branch'], p['w_merge'], p['w_out'])
    return y_ctx, y_lat

def ec_moe(h, w_router, w_g, w_u, w_d):
    b, n, _ = h.shape
    cap = CAPACITY_FACTOR * n // N_EXPERTS
    aff = jax.nn.softmax((h @ w_router).astype(F32), axis=-1)
    vals, idx = lax.top_k(jnp.swapaxes(aff, 1, 2), cap)
    bidx = jnp.arange(b)[:, None, None]
    xe = h[bidx, idx]
    act = jax.nn.silu(jnp.einsum('becd,edf->becf', xe, w_g)) * jnp.einsum('becd,edf->becf', xe, w_u)
    ye = jnp.einsum('becf,efd->becd', act, w_d) * vals[..., None].astype(h.dtype)
    return jnp.zeros_like(h).at[bidx, idx].add(ye)

def hybrid_layer(x_ctx, x_lat, mod_ctx, mod_lat, p, lb_f, lb_b, cos, sin, need_ctx):
    sh_c, sc_c, gt_c, shf_c, scf_c, gtf_c = jnp.split(mod_ctx, 6, axis=-1)
    sh_l, sc_l, gt_l, shf_l, scf_l, gtf_l = jnp.split(mod_lat, 6, axis=-1)
    h_ctx = modulate(rmsnorm(x_ctx, p['g_pre_mix']), sh_c, sc_c)
    h_lat = modulate(rmsnorm(x_lat, p['g_pre_mix']), sh_l, sc_l)
    y_ctx, y_lat = token_mixer(h_ctx, h_lat, p, lb_f, lb_b, cos, sin, need_ctx)
    x_lat = x_lat + gt_l * rmsnorm(y_lat, p['g_post_mix'])
    f_lat = ec_moe(modulate(rmsnorm(x_lat, p['g_pre_ffn']), shf_l, scf_l),
                   p['w_router'], p['w_exp_gate'], p['w_exp_up'], p['w_exp_down'])
    x_lat = x_lat + gtf_l * rmsnorm(f_lat, p['g_post_ffn'])
    if not need_ctx:
        return None, x_lat
    x_ctx = x_ctx + gt_c * rmsnorm(y_ctx, p['g_post_mix'])
    f_ctx = ec_moe(modulate(rmsnorm(x_ctx, p['g_pre_ffn']), shf_c, scf_c),
                   p['w_router'], p['w_exp_gate'], p['w_exp_up'], p['w_exp_down'])
    x_ctx = x_ctx + gtf_c * rmsnorm(f_ctx, p['g_post_ffn'])
    return x_ctx, x_lat

def hgrn_lower_bounds(logits):
    pr = jax.nn.softmax(logits.astype(F32), axis=1)
    return jnp.cumsum(pr, axis=1) - pr[:, :1]

def setup_inputs(seed: int = 0) -> dict:
    key = jax.random.key(seed)
    ks = jax.random.split(key, 32)
    D, F, E = D_MODEL, EXPERT_FF, N_EXPERTS

    def nrm(k, shape, scale):
        return jax.random.normal(k, shape, F32) * scale

    def gain(k, shape):
        return 1.0 + 0.05 * jax.random.normal(k, shape, F32)

    dt = jnp.exp(jax.random.uniform(ks[18], (DEPTH, 2, GDN_HEADS), F32, math.log(1e-3), math.log(1e-1)))
    return {
        'x': nrm(ks[0], (BATCH, SEQ, D), 1.0),
        'c': nrm(ks[1], (BATCH, D), 1.0),
        'ctx': nrm(ks[2], (BATCH, CTX_LEN, D), 1.0),
        'c_ctx': nrm(ks[3], (D,), 1.0),
        'w_ada': nrm(ks[4], (DEPTH, D, 6 * D), 0.5 * D ** -0.5),
        'b_ada': nrm(ks[5], (DEPTH, 6 * D), 0.02),
        'g_pre_mix': gain(ks[6], (DEPTH, D)),
        'g_post_mix': gain(ks[7], (DEPTH, D)),
        'g_pre_ffn': gain(ks[8], (DEPTH, D)),
        'g_post_ffn': gain(ks[9], (DEPTH, D)),
        'w_in': nrm(ks[10], (DEPTH, D, D_IN), D ** -0.5),
        'ret_norm_g': gain(ks[11], (DEPTH, HEAD_DIM)),
        'hg_lb_logits': nrm(ks[12], (2, DEPTH, HG_HEADS * HEAD_DIM), 1.0),
        'hg_norm_g': gain(ks[13], (DEPTH, HEAD_DIM)),
        'at_q_norm_g': gain(ks[14], (DEPTH, HEAD_DIM)),
        'at_k_norm_g': gain(ks[15], (DEPTH, HEAD_DIM)),
        'gd_conv_w': nrm(ks[16], (DEPTH, CONV_W, 3 * GDN_HEADS * HEAD_DIM), CONV_W ** -0.5),
        'gd_a_log': jnp.log(jax.random.uniform(ks[17], (DEPTH, 2, GDN_HEADS), F32, 1.0, 16.0)),
        'gd_dt_bias': dt + jnp.log(-jnp.expm1(-dt)),
        'gd_norm_g': gain(ks[19], (DEPTH, HEAD_DIM)),
        'w_branch': nrm(ks[20], (DEPTH, N_BRANCHES, BRANCH_W, D), BRANCH_W ** -0.5),
        'w_merge': nrm(ks[21], (DEPTH, N_BRANCHES, D, D), D ** -0.5),
        'w_out': nrm(ks[22], (DEPTH, D, D), D ** -0.5),
        'w_router': nrm(ks[23], (DEPTH, D, E), D ** -0.5),
        'w_exp_gate': nrm(ks[24], (DEPTH, E, D, F), D ** -0.5),
        'w_exp_up': nrm(ks[25], (DEPTH, E, D, F), D ** -0.5),
        'w_exp_down': nrm(ks[26], (DEPTH, E, F, D), F ** -0.5),
    }

def reference(x, c, ctx, c_ctx, w_ada, b_ada, g_pre_mix, g_post_mix, g_pre_ffn, g_post_ffn, w_in,
              ret_norm_g, hg_lb_logits, hg_norm_g, at_q_norm_g, at_k_norm_g, gd_conv_w, gd_a_log,
              gd_dt_bias, gd_norm_g, w_branch, w_merge, w_out, w_router, w_exp_gate, w_exp_up, w_exp_down):
    cos, sin = axial_rope_tables(x.shape[1])
    lower = hgrn_lower_bounds(hg_lb_logits)
    x_ctx, x_lat = ctx, x
    for l in range(DEPTH):
        p = {
            'w_in': w_in[l], 'ret_norm_g': ret_norm_g[l], 'hg_norm_g': hg_norm_g[l],
            'at_q_norm_g': at_q_norm_g[l], 'at_k_norm_g': at_k_norm_g[l], 'gd_conv_w': gd_conv_w[l],
            'gd_a_log': gd_a_log[l], 'gd_dt_bias': gd_dt_bias[l], 'gd_norm_g': gd_norm_g[l],
            'w_branch': w_branch[l], 'w_merge': w_merge[l], 'w_out': w_out[l], 'w_router': w_router[l],
            'w_exp_gate': w_exp_gate[l], 'w_exp_up': w_exp_up[l], 'w_exp_down': w_exp_down[l],
            'g_pre_mix': g_pre_mix[l], 'g_post_mix': g_post_mix[l],
            'g_pre_ffn': g_pre_ffn[l], 'g_post_ffn': g_post_ffn[l],
        }
        mod_lat = (jax.nn.silu(c) @ w_ada[l] + b_ada[l])[:, None, :]
        mod_ctx = (jax.nn.silu(c_ctx) @ w_ada[l] + b_ada[l])[None, None, :]
        x_ctx, x_lat = hybrid_layer(x_ctx, x_lat, mod_ctx, mod_lat, p, lower[0, l], lower[1, l],
                                    cos, sin, l < DEPTH - 1)
    return x_lat


_drawn_inputs = setup_inputs


def setup_inputs(seed=0):
    import zlib

    import numpy as np

    out = dict(_drawn_inputs(seed))
    spreads = {}
    factors = {'at_q_norm_g': 3.705, 'at_k_norm_g': 3.202}
    for name, (base, spread) in spreads.items():
        noise = np.random.default_rng([zlib.crc32(name.encode()), seed]).standard_normal(out[name].shape)
        drawn = base * np.exp(spread * noise) if base else spread * noise
        out[name] = __import__('jax').numpy.asarray(drawn.astype(out[name].dtype))
    for name, factor in factors.items():
        out[name] = (out[name] * factor).astype(out[name].dtype)
    return out
```

```python
from contextlib import ExitStack

import numpy as np

import concourse.bass as bass
from concourse import mybir

F32 = mybir.dt.float32
BF16 = mybir.dt.bfloat16
U16 = mybir.dt.uint16
U32 = mybir.dt.uint32
ACT = mybir.ActivationFunctionType
ALU = mybir.AluOpType
AX = mybir.AxisListType

P = 128
D = 1024
SEQ = 512
CTX = 256
TOK = CTX + SEQ
DEPTH = 2
GRID_W = 64
HD = 64
HEADS = 4
BW = HEADS * HD
EXPERTS = 16
FF = 1024
EPS = 1e-6
KB = D // P
NT = TOK // P
CT = CTX // P
CAP_LAT = 2 * SEQ // EXPERTS
CAP_CTX = 2 * CTX // EXPERTS
QSCALE = HD ** -0.5
FWD_ORDER = [0, 1, 2, 3, 4, 5]
BWD_ORDER = [1, 0, 5, 4, 3, 2]
ORDERS = [FWD_ORDER, BWD_ORDER]

RET0, HG0, AT0, GDF0, GDT0, D_IN = 0, 1024, 2304, 2816, 3584, 3856
SLOTW = 512
GROUP_SLOTS = {
    "ret": [(0, 512), (512, 512)],
    "hg": [(1024, 512), (1536, 512), (2048, 256)],
    "at": [(2304, 512)],
    "gd": [(3584, 272), (2816, 512), (3328, 256)],
}
CHP = TOK + 4


def tok_tile(i):
    return slice(P * i, P * i + P)


def hpos(h):
    return 2 * (h % 2) + h // 2


def constants():
    u = np.arange(P)[:, None]
    t = np.arange(P)[None, :]
    cols, at = [], {}

    def put(name, a):
        a = np.asarray(a, np.float32).reshape(P, -1)
        at[name] = (sum(c.shape[1] for c in cols), a.shape[1])
        cols.append(a)

    put("ident", np.eye(P))
    for d in range(2):
        run = (u <= t) if d == 0 else (u >= t)
        parts = [run]
        for half in (64, 32):
            edge = (t // (2 * half)) * 2 * half + half
            right = t >= edge
            if d == 0:
                m = np.where(right, (u >= edge) & (u <= t), (u > t) & (u < edge))
            else:
                m = np.where(right, (u >= edge) & (u < t), (u >= t) & (u < edge))
            parts.append(m)
        edge = (t // 32) * 32 + 16
        if d == 0:
            m = np.where(t >= edge, 1.0 * ((u >= edge) & (u <= t)), -1.0 * ((u > t) & (u < edge)))
        else:
            m = np.where(t < edge, 1.0 * ((u >= t) & (u < edge)), -1.0 * ((u >= edge) & (u < t)))
        parts.append(m)
        put(f"sums{d}", np.concatenate([1.0 * p for p in parts], 1))
    for d in range(2):
        put(f"tail{d}", (u > t) if d == 0 else (u < t))
    put("ones", np.ones((P, P)))
    lg = np.log1p(-np.exp2(-5.0 - np.arange(HEADS)))
    lgd = [lg, lg[::-1]]
    s = u
    dr = np.zeros((P, HEADS, P))
    for h in range(HEADS):
        dr[:, hpos(h)] = (np.where(s <= t, np.exp(lgd[0][h] * np.maximum(t - s, 0)), 0)
                    + np.where(s >= t, np.exp(lgd[1][h] * np.maximum(s - t, 0)), 0)) * QSCALE
    put("ret_decay", dr)
    qd = np.zeros((P, 2, 2, P))
    cd = np.zeros((P, 2, 2))
    for d in range(2):
        for pair in range(2):
            for half in range(2):
                g = lgd[d][2 * pair + half]
                dist = (t[0] + 1) if d == 0 else (P - t[0])
                qd[64 * half:64 * half + 64, d, pair] = np.exp(g * dist)
                cd[64 * half:64 * half + 64, d, pair] = np.exp(g * P)
    put("ret_qdec", qd)
    put("ret_cdec", cd)
    kd = np.zeros((P, 2, HEADS))
    for d in range(2):
        for h in range(HEADS):
            dist = (P - 1 - u[:, 0]) if d == 0 else u[:, 0]
            kd[:, d, h] = np.exp(lgd[d][h] * dist) * QSCALE
    put("ret_kdec", kd)
    tok = np.arange(SEQ)
    inv = 10000.0 ** (-np.arange(0, 32, 2) / 32)
    ang = np.stack([(tok // GRID_W)[:, None] * inv, (tok % GRID_W)[:, None] * inv], 1)
    for name, f in (("cos", np.cos), ("sin", np.sin)):
        put(name, f(ang).reshape(SEQ // P, P, 32).transpose(1, 0, 2))
    put("eye2", np.concatenate([np.eye(64), np.eye(64)], 0))
    put("sel", (u % 32 == t[:, 0:2]))
    put("eps", np.full((P, 1), EPS))
    f32 = np.ascontiguousarray(np.concatenate(cols, 1))
    masks = []
    for d in range(2):
        for b in (1, 2, 4, 8, 16, 32, 64):
            first, second = (s, t) if d == 0 else (t, s)
            masks.append((first // (2 * b) == second // (2 * b)) & (first // b % 2 == 0) & (second // b % 2 == 1))
    ONE_BF16 = 0x3F80
    bits = np.ascontiguousarray(np.where(np.concatenate(masks, 1), ONE_BF16, 0).astype(np.uint16))
    return f32, bits, at


def out_tiles(L):
    return list(range(NT)) if L < DEPTH - 1 else list(range(CT, NT))


def proj_jobs(c0, w):
    if GDF0 <= c0 < GDT0:
        return [(f, s) for f in range(w // P) for s in range(2)]
    return list(range(NT))


MOD_ITEMS = 6 * D // SLOTW


class Plan:

    def __init__(self):
        self.items, self.item_no, self.item_free = [], {}, {}
        self.job_no, self.proj_no, self.proj_end = {}, {}, {}
        self.jobs = self.proj = 0
        self.start, self.experts = [], []
        for L in range(DEPTH):
            self.start.append(len(self.items))
            if L == 0:
                self.modulation(0)
            for g in ("ret", "hg", "at", "gd"):
                for s, (c0, w) in enumerate(GROUP_SLOTS[g]):
                    self.item(L, g, s)
                    for j in proj_jobs(c0, w):
                        self.job(L, g, s, j)
                        self.proj_no[L, g, s, j] = self.proj
                        self.proj += 1
                    self.free(L, g, s)
                self.proj_end[L, g] = self.proj
            if L + 1 < DEPTH:
                self.modulation(L + 1)
            for n in range(4):
                for half in range(2):
                    self.item(L, "merge", n, half)
                    for i in out_tiles(L):
                        self.job(L, "merge", n, half, i)
                        self.job(L, "branch", n, half, i)
                    self.free(L, "merge", n, half)
            self.item(L, "out", 0)
            self.item(L, "out", 1)
            for i in out_tiles(L):
                for half in range(2):
                    self.job(L, "out", i, half)
            self.free(L, "out", 0)
            self.free(L, "out", 1)
            self.experts.append(len(self.items))
            for e in range(EXPERTS):
                for j in range(6):
                    self.item(L, "moe", e, j)
                    self.job(L, "moe", e, j)
                    self.free(L, "moe", e, j)

    def modulation(self, L):
        for c in range(MOD_ITEMS):
            self.item(L, "ada", c)
            self.job(L, "ada", c)
            self.free(L, "ada", c)

    def item(self, *key):
        self.item_no[key] = len(self.items)
        self.items.append(key)

    def job(self, *key):
        self.jobs += 1
        self.job_no[key] = self.jobs

    def free(self, *key):
        self.item_free[self.item_no[key]] = self.jobs


RING = 3

PER_LAYER = {
    "at_exp": 24, "at_max": 24, "at_normed": 1, "at_pt": 24, "at_pturn": 24, "at_pv": 24, "at_roped": 1,
    "at_rs": 1, "at_scores": 24, "at_sq": 1, "at_ss": 1, "at_turn": 6, "at_turn_evac": 6, "at_ytile": 6,
    "gd_abs": 1, "gd_am": 84, "gd_at": 12, "gd_conv": 1, "gd_cum": 1, "gd_cv": 6, "gd_cve": 6,
    "gd_evac_act": 12, "gd_evac_dve": 12, "gd_fin": 12, "gd_ga": 12, "gd_gam": 12, "gd_gate": 1, "gd_gm": 12,
    "gd_nea_exp": 1, "gd_pads": 1, "gd_pm": 12, "gd_pmm": 12, "gd_qkn": 6, "gd_rs": 6, "gd_scan": 10,
    "gd_scan_mm": 8, "gd_scores": 6, "gd_silu": 6, "gd_solved": 12, "gd_sp": 1, "gd_sq": 6, "gd_ss": 6,
    "gd_sums": 1, "gd_tiled": 6, "gd_tu": 72, "gd_turn": 6, "gd_turn2": 6, "gd_turn2_evac": 6, "gd_uw": 12,
    "gd_uws": 12, "gd_x": 84, "gd_xe": 72, "gd_y": 72, "hg_eb": 6, "hg_ee": 12, "hg_fac_dve": 12,
    "hg_fac_pool": 12, "hg_kb": 6, "hg_lf": 1, "hg_mc": 12, "hg_own": 6, "hg_own_evac": 6, "hg_pm": 12,
    "hg_pmsum": 6, "hg_pt": 12, "hg_q": 1, "hg_qx": 12, "hg_sigmoids": 1, "hg_sums": 12, "hg_tail": 6,
    "hg_turn": 6, "hg_turn_evac": 6, "hg_z": 1, "merge_sum": 36, "n1_evac_act": 6, "n1_evac_dve": 6,
    "n1_rstd": 1, "n1_turned": 6, "ret_kdec": 1, "ret_own": 6, "ret_own_evac": 6, "ret_pm": 6, "ret_qx": 6,
    "ret_roped": 1, "ret_scores": 6, "ret_turn": 6, "ret_turn_evac": 6, "row_diag": 8, "row_evac": 8,
    "row_mm": 8, "xn_done": 6,
}


def build(nc, A, out):
    plan = Plan()
    ctx = ExitStack()
    with ctx:
        def sb(name, shape, dt=F32):
            return ctx.enter_context(nc.sbuf_tensor(name, shape, dt))

        def ended(what, L, g):
            n = 0
            for L2 in range(DEPTH):
                for g2 in ("ret", "hg", "at", "gd"):
                    if (L2, g2) == (L, g):
                        return n
                    nt = len(out_tiles(L2))
                    per = {"inter": nt, "osum": nt, "yturn": nt, "yevac": nt - 1, "y": 1, "yT": 1}
                    if g2 == "at":
                        per.update(inter=0, osum=0)
                    n += per.get(what, 0 if g2 == "at" else 1)

        def before(L, what):
            return L * PER_LAYER[what]

        sems = {}

        def sem(name):
            if name not in sems:
                sems[name] = ctx.enter_context(nc.semaphore(name))
            return sems[name]

        tables, masks, at = A["tables"], A["merge_masks"], A["table_at"]
        cst = sb("cst", [P, tables.shape[1]])
        ring = sb("ring", [P, RING, KB, SLOTW])
        hT = sb("hT", [P, KB, TOK])
        regA = sb("regA", [P, 7680])
        regB = sb("regB", [P, 7680])
        regC = sb("regC", [P, 3072])
        yT = sb("yT", [P, 2 * 4, TOK])
        regQ = sb("regQ", [P, 3072])
        vecs = sb("vecs", [P, 4, DEPTH, KB])
        badaT = sb("badaT", [P, DEPTH, 48])
        convT = sb("convT", [P, DEPTH, 3, 6])
        csil = sb("csil", [P, KB, 32])
        modraw = sb("modraw", [P, 96])
        gains = sb("gains", [P, 5, DEPTH, HD])
        alog = sb("alog", [P, DEPTH, 8])
        dtb = sb("dtb", [P, DEPTH, 8])
        modv = sb("modv", [P, 48, 2])
        wrt = sb("wrt", [P, KB, EXPERTS])
        T = sb("T", [P, 2048])
        small = sb("small", [P, 512])
        psum = ctx.enter_context(nc.psum_tensor("psum", [P, 8, 512], F32))

        def tab(name):
            o, n = at[name]
            return cst[:, o:o + n]

        ident, ones, eps_col = tab("ident"), tab("ones"), tab("eps")
        run = [tab(f"sums{d}")[:, 0:P] for d in range(2)]
        sums = [tab(f"sums{d}") for d in range(2)]
        tail = [tab(f"tail{d}") for d in range(2)]

        def dram(name, shape):
            return nc.dram_tensor(name, shape, F32, kind="Internal").ap()

        out_toks = [P * len(out_tiles(L)) for L in range(DEPTH)]
        xn_ffn = [dram(f"xn_ffn{L}", [out_toks[L], D]) for L in range(DEPTH)]
        ffn = [dram(f"ffn{L}", [out_toks[L], D]) for L in range(DEPTH)]
        x_end = dram("x_end", [TOK, D])

        def x_in(L, i):
            if L:
                return x_end[P * i:P * i + P, :]
            return A["ctx"][0, P * i:P * i + P, :] if i < CT else A["x"][0, P * (i - CT):P * (i - CT) + P, :]

        def ps(b, w=512, p=slice(0, P)):
            return psum[p, b, 0:w]

        def heads(ap, n=HEADS):
            return ap.rearrange("p (h c) -> p h c", h=n)

        def bc_mid(ap, n):
            return ap.unsqueeze(1).to_broadcast([ap.shape[0], n, ap.shape[1]])

        def bc_in(ap, n):
            return ap.unsqueeze(2).to_broadcast([ap.shape[0], ap.shape[1], n])

        half_of = lambda h: slice(64 * (h % 2), 64 * (h % 2) + 64)

        P1 = regA[:, 0:6144].rearrange("p (t c) -> p t c", t=NT)
        P2 = regB[:, 0:7680].rearrange("p (t c) -> p t c", t=NT)
        P3 = regA[:, 0:3072].rearrange("p (t c) -> p t c", t=NT)
        FM = regA[:, 0:6 * CHP].rearrange("p (f t) -> p f t", f=6)
        P4 = regA[:, 6 * CHP:6 * CHP + 1632].rearrange("p (t c) -> p t c", t=NT)
        DS = regC[:, 0:1536].rearrange("p (t d c) -> p t d c", t=NT, d=2)
        SST = regC[:, 1536:3072].rearrange("p (t d c) -> p t d c", t=NT, d=2)
        C0, C1 = regC[:, 0:1536], regC[:, 1536:3072]
        O_of = {"ret": P1[:, :, 512:768], "hg": P2[:, :, 512:768],
                "gd": regB[:, 0:1536].rearrange("p (t c) -> p t c", t=NT)}
        QX_of = {"ret": P1[:, :, 0:512].rearrange("p t (d c) -> p t d c", d=2),
                 "hg": P2[:, :, 0:512].rearrange("p t (d c) -> p t d c", d=2),
                 "gd": regQ[:, :].rearrange("p (t d c) -> p t d c", t=NT, d=2)}
        G_of = {"ret": P1[:, :, 768:1024], "hg": P2[:, :, 1024:1280], "gd": P4[:, :, 16:272]}
        BR = {"ret": 0, "hg": 1, "at": 2, "gd": 3}
        GAIN = {"ret": 0, "hg": 1, "gd": 2}
        MT = regB[:, 1536:3072].rearrange("p (t d c) -> p t d c", t=NT, d=2)
        DEC = small[:, 0:24].rearrange("p (t d c) -> p t d c", t=NT, d=2)
        M = regA[:, 0:6144].rearrange("p (t c) -> p t c", t=NT)
        GROW = regB[:, 0:4096].rearrange("p (w s c) -> p w s c", w=2, s=2)

        def load_list():
            rows = T
            L_ = [(cst[:, :], tables)]
            for v, name in enumerate(("g_pre_mix", "g_post_mix", "g_pre_ffn", "g_post_ffn")):
                L_.append((rows[16 * v:16 * v + 16, 0:P], A[name].rearrange("l (k p) -> (l k) p", p=P)))
            L_.append((rows[0:96, P:2 * P], A["b_ada"].rearrange("l (k p) -> (l k) p", p=P)))
            L_.append((rows[0:36, 2 * P:3 * P], A["gd_conv_w"].rearrange("l w (k p) -> (l w k) p", p=P)))
            L_.append((rows[0:8, 3 * P:4 * P], A["c_ctx"].rearrange("(k p) -> k p", p=P)))
            L_.append((rows[8:16, 3 * P:4 * P], A["c"][0, :].rearrange("(k p) -> k p", p=P)))
            for g, name in enumerate(("ret_norm_g", "hg_norm_g", "gd_norm_g", "at_q_norm_g", "at_k_norm_g")):
                L_.append((gains[:, g].rearrange("p l c -> p (l c)"),
                           A[name].rearrange("l c -> (l c)").partition_broadcast(P)))
            L_.append((alog[:, :].rearrange("p l c -> p (l c)"),
                       A["gd_a_log"].rearrange("l d c -> (l d c)").partition_broadcast(P)))
            L_.append((dtb[:, :].rearrange("p l c -> p (l c)"),
                       A["gd_dt_bias"].rearrange("l d c -> (l d c)").partition_broadcast(P)))
            return L_

        N_SETUP = len(load_list())

        def setup_sp(sp):
            for dst, src in load_list():
                sp.dma_start(dst, src).then_inc(sem("setup_loaded"), 16)

        def setup_pe(pe):
            pe.wait_ge(sem("setup_loaded"), 16 * N_SETUP)
            for k, n in enumerate((64, 96, 36, 16)):
                nc.tensor.transpose(psum[:, k, 0:n], T[0:n, P * k:P * k + P], ident[0:n, 0:n]).then_inc(sem("setup_turned"), 1)

        def setup_dve(dve):
            dve.wait_ge(sem("setup_turned"), 4)
            nc.vector.tensor_copy(vecs[:, :, :, :].rearrange("p v l k -> p (v l k)"), ps(0, 64)).then_inc(sem("vecs_ready"), 1)
            nc.vector.tensor_copy(badaT[:, :, :].rearrange("p l k -> p (l k)"), ps(1, 96)).then_inc(sem("vecs_ready"), 1)
            nc.vector.tensor_copy(convT[:, :, :, :].rearrange("p l w k -> p (l w k)"), ps(2, 36)).then_inc(sem("vecs_ready"), 1)
            dve.wait_ge(sem("c_sigmoid"), 1)
            dchain(nc.vector.memset(csil[:, :, :], 0.0))
            for s in range(2):
                ins = nc.vector.tensor_tensor(csil[:, :, s], ps(3, 16)[:, 8 * s:8 * s + 8], small[:, 8 * s:8 * s + 8], ALU.mult)
                ins.then_inc(sem("vecs_ready"), 1)

        def setup_act(act):
            act.wait_ge(sem("setup_turned"), 4)
            nc.scalar.activation(small[:, 0:16], ps(3, 16), ACT.Sigmoid).then_inc(sem("c_sigmoid"), 1)

        def weight_ap(key):
            L, kind = key[0], key[1]
            if kind == "ada":
                c = key[2]
                return A["w_ada"][L].rearrange("(k p) n -> p k n", p=P)[:, :, SLOTW * c:SLOTW * c + SLOTW]
            if kind in GROUP_SLOTS:
                c0, w = GROUP_SLOTS[kind][key[2]]
                return A["w_in"][L].rearrange("(k p) n -> p k n", p=P)[:, :, c0:c0 + w]
            half = key[-1]
            cols = slice(SLOTW * half, SLOTW * half + SLOTW)
            if kind == "merge":
                return A["w_merge"][L, key[2]].rearrange("(k p) n -> p k n", p=P)[:, :, cols]
            if kind == "out":
                return A["w_out"][L].rearrange("(k p) n -> p k n", p=P)[:, :, cols]

        def moe_weight_ap(L, e, j):
            w = (A["w_exp_gate"], A["w_exp_up"], A["w_exp_gate"], A["w_exp_up"], A["w_exp_down"], A["w_exp_down"])[j]
            half = (0, 0, 1, 1, 0, 1)[j]
            return w[L, e].rearrange("(k p) n -> p k n", p=P)[:, :, SLOTW * half:SLOTW * half + SLOTW]

        def slot_of(n):
            return n % RING

        def loaded_value(n):
            return 16 * (n // RING + 1)

        def stream_sp(sp, L):
            for n in range(plan.start[L], plan.experts[L]):
                key = plan.items[n]
                if n >= RING:
                    sp.wait_ge(sem("jobs_done"), plan.item_free[n - RING])
                src = weight_ap(key)
                dst = ring[:, slot_of(n), 0:src.shape[1], 0:src.shape[2]]
                sp.dma_start(dst, src).then_inc(sem(f"slot{slot_of(n)}_loaded"), 16)
                if key[1] == "merge":
                    for r in {0: [], 1: [0, 1]}.get(2 * key[2] + key[3], [2 * key[2] + key[3]]):
                        load_branch(sp, L, r // 2, r % 2)

        def w_branch(half):
            return T[:, D * half:D * half + D].rearrange("p (k c) -> p k c", k=2)

        def load_branch(sp, L, n, half):
            if n == 0:
                sp.wait_ge(sem("yT"), ended("yT", L, "gd") + 1)
            else:
                sp.wait_ge(sem("jobs_done"), plan.job_no[L, "branch", n - 1, half, NT - 1])
            sp.dma_start(w_branch(half), A["w_branch"][L, n].rearrange("(k p) n -> p k n", p=P)[:, :, SLOTW * half:SLOTW * half + SLOTW]).then_inc(sem(f"branch{half}_loaded"), 16)

        def moe_sp(sp, L):
            n0 = plan.item_no[L, "moe", 0, 0]
            j0 = plan.job_no[L, "moe", 0, 0] - 1
            for j in range(RING):
                sp.wait_ge(sem("jobs_done"), plan.item_free[n0 + j - RING])
                sp.dma_start(ring[:, slot_of(n0 + j)], moe_weight_ap(L, 0, j)).then_inc(sem(f"slot{slot_of(n0 + j)}_loaded"), 16)
            for j in range(RING, 6):
                sp.wait_ge(sem("jobs_done"), j0 + j - RING + 1)
                sp.dma_start(ring[:, slot_of(n0 + j)], moe_weight_ap(L, 0, j)).then_inc(sem(f"slot{slot_of(n0 + j)}_loaded"), 16)
            with sp.Fori(1, EXPERTS) as e:
                for j in range(6):
                    sp.wait_ge(sem("jobs_done"), e * 6 + (j0 + j - RING + 1))
                    sp.dma_start(ring[:, slot_of(n0 + j)], moe_weight_ap(L, e, j)).then_inc(sem(f"slot{slot_of(n0 + j)}_loaded"), 16)

        def wait_item(pe, *key):
            n = plan.item_no[key]
            pe.wait_ge(sem(f"slot{slot_of(n)}_loaded"), loaded_value(n))
            return ring[:, slot_of(n)]

        MODP = yT[:, 7, TOK - SLOTW:TOK]

        def mod_mm(pe, L, c):
            w = wait_item(pe, L, "ada", c)
            if L or c:
                pe.wait_ge(sem("mod_evac"), MOD_ITEMS * L + c)
            for k in range(KB):
                g = 32 * (k % 4)
                ins = nc.tensor.matmul(psum[g:g + 32, 0, :], csil[:, k, :], w[:, k, :], start=(k < 4), stop=(k >= 4))
            ins.then_inc(sem("jobs_done"), 1)

        def mod_turn(pe, L, c):
            pe.wait_ge(sem("mod_evac"), MOD_ITEMS * L + c + 1)
            for f in range(4):
                o = 2 * (4 * c + f)
                ins = nc.tensor.matmul(psum[:, 1, o:o + 2], MODP[:, P * f:P * f + P], tab("sel"), start=True, stop=True)
            ins.then_inc(sem("mod_turned"), 1)

        def mod_pe(pe, L):
            pe.wait_ge(sem("vecs_ready"), 5)
            for c in range(MOD_ITEMS):
                mod_mm(pe, L, c)
                if c:
                    mod_turn(pe, L, c - 1)
            mod_turn(pe, L, MOD_ITEMS - 1)

        def mod_evac(act, L, c):
            act.wait_ge(sem("jobs_done"), plan.job_no[L, "ada", c])
            if L or c:
                act.wait_ge(sem("mod_turned"), MOD_ITEMS * L + c)
            nc.scalar.activation(MODP, ps(0), ACT.Copy).then_inc(sem("mod_evac"), 1)

        def mod_keep(act, L):
            act.wait_ge(sem("mod_turned"), MOD_ITEMS * (L + 1))
            if L:
                act.wait_ge(sem("mod_ready"), L)
            nc.scalar.activation(modraw[:, :], ps(1, 96), ACT.Copy).then_inc(sem("mod_raw"), 1)

        def mod_act(act, L):
            for c in range(MOD_ITEMS):
                mod_evac(act, L, c)
            mod_keep(act, L)

        def mod_dve(dve, L):
            dve.wait_ge(sem("mod_raw"), L + 1)
            dve.wait_ge(sem("vecs_ready"), 3)
            if L:
                dve.wait_ge(sem("xeT_ready"), (EXPERTS + 1) * L)
            dchain(nc.vector.tensor_tensor(modv[:, :, :], modraw[:, :].rearrange("p (k s) -> p k s", s=2),
                                           bc_in(badaT[:, L, :], 2), ALU.add))
            for part, v in ((1, 0), (4, 2)):
                m = modv[:, 8 * part:8 * part + 8, :]
                dchain(nc.vector.tensor_scalar(m, m, 1.0, None, ALU.add))
                dchain(nc.vector.tensor_tensor(m, m, bc_in(vecs[:, v, L, :], 2), ALU.mult))
            for part, v in ((2, 1), (5, 3)):
                m = modv[:, 8 * part:8 * part + 8, :]
                ins = nc.vector.tensor_tensor(m, m, bc_in(vecs[:, v, L, :], 2), ALU.mult)
                if part == 2:
                    dchain(ins)
            ins.then_inc(sem("mod_ready"), 1)

        def XF(i):
            return (regC, regQ)[i // 3][:, D * (i % 3):D * (i % 3) + D]

        def XN(i):
            return regA[:, D * i:D * i + D]

        stat = sb("stat", [P, 64])

        def norm_pool(pool, L):
            for i in range(NT):
                pool.dma_start(XF(i), x_in(L, i)).then_inc(sem("x_loaded"), 16)

        def norm_stats_act(act, L):
            for i in range(NT):
                if L:
                    act.wait_ge(sem("post_done"), NT * (L - 1) + i + 1)
                else:
                    act.wait_ge(sem("x_loaded"), 16 * NT)
                ins = nc.scalar.activation(XN(i), XF(i), ACT.Square, accum_out=stat[:, i:i + 1])
            achain(ins)
            achain(nc.scalar.activation(stat[:, 8:8 + NT], stat[:, 0:NT], ACT.Ln, bias=eps_col, scale=1.0 / D))
            nc.scalar.activation(stat[:, 16:16 + NT], stat[:, 8:8 + NT], ACT.Exp, scale=-0.5).then_inc(sem("n1_rstd"), 1)

        def norm_act(act, L):
            for i in range(NT):
                norm_evac_act(act, L, i)

        def norm_evac_act(act, L, i):
            act.wait_ge(sem("n1_turned"), before(L, "n1_turned") + i + 1)
            act.wait_ge(sem("mod_ready"), L + 1)
            s = 0 if i < CT else 1
            for j in range(4):
                k = 4 + j
                ins = nc.scalar.activation(hT[:, k, tok_tile(i)], psum[:, 3 + 2 * (i % 2), P * j:P * j + P], ACT.Identity,
                                           bias=modv[:, k, s:s + 1], scale=modv[:, 8 + k, s:s + 1])
            ins.then_inc(sem("n1_evac_act"), 1)

        def norm_scale_dve(dve, L):
            dve.wait_ge(sem("n1_rstd"), before(L, "n1_rstd") + 1)
            for i in range(NT):
                nc.vector.tensor_scalar(XN(i), XF(i), stat[:, 16 + i:17 + i], None, ALU.mult).then_inc(sem("xn_done"), 1)

        def norm_dve(dve, L):
            for i in range(NT):
                norm_evac_dve(dve, L, i)

        def norm_evac_dve(dve, L, i):
            dve.wait_ge(sem("n1_turned"), before(L, "n1_turned") + i + 1)
            if i == 0:
                dve.wait_ge(sem("mod_ready"), L + 1)
            s = 0 if i < CT else 1
            for j in range(4):
                ins = nc.vector.tensor_scalar(hT[:, j, tok_tile(i)], psum[:, 2 + 2 * (i % 2), P * j:P * j + P],
                                              modv[:, 8 + j, s:s + 1], modv[:, j, s:s + 1], ALU.mult, ALU.add)
            ins.then_inc(sem("n1_evac_dve"), 1)

        def norm_pe(pe, L):
            for i in range(NT):
                pe.wait_ge(sem("xn_done"), before(L, "xn_done") + i + 1)
                if i >= 2:
                    pe.wait_ge(sem("n1_evac_act"), before(L, "n1_evac_act") + i - 1)
                    pe.wait_ge(sem("n1_evac_dve"), before(L, "n1_evac_dve") + i - 1)
                for k in range(KB):
                    ins = nc.tensor.transpose(psum[:, 2 + 2 * (i % 2) + k // 4, P * (k % 4):P * (k % 4) + P],
                                              XN(i)[:, P * k:P * k + P], ident)
                ins.then_inc(sem("n1_turned"), 1)

        def proj_pe(pe, L, g):
            pe.wait_ge(sem("n1_evac_act"), before(L, "n1_evac_act") + NT)
            pe.wait_ge(sem("n1_evac_dve"), before(L, "n1_evac_dve") + NT)
            for s, (c0, w) in enumerate(GROUP_SLOTS[g]):
                wt = wait_item(pe, L, g, s)
                for j in proj_jobs(c0, w):
                    n = plan.proj_no[L, g, s, j]
                    if n >= 2:
                        pe.wait_ge(sem("proj_evac"), n - 1)
                    for k in range(KB):
                        if isinstance(j, tuple):
                            f, st = j
                            toks = slice(0, CTX) if st == 0 else slice(CTX, TOK)
                            ins = nc.tensor.matmul(ps(n % 2, toks.stop - toks.start), wt[:, k, P * f:P * f + P],
                                                   hT[:, k, toks], start=(k == 0), stop=(k == KB - 1))
                        else:
                            ins = nc.tensor.matmul(ps(n % 2, w), hT[:, k, tok_tile(j)], wt[:, k, 0:w],
                                                   start=(k == 0), stop=(k == KB - 1))
                    ins.then_inc(sem("jobs_done"), 1)

        def proj_act(act, L, g):
            dest = {"ret": P1, "hg": P2, "at": P3, "gd": P4}[g]
            base = {"ret": RET0, "hg": HG0, "at": AT0, "gd": GDT0}[g]
            if g == "at":
                act.wait_ge(sem("yT"), ended("yT", L, "ret") + 1)
            elif g == "gd":
                act.wait_ge(sem("yT"), ended("yT", L, "at") + 1)
            for s, (c0, w) in enumerate(GROUP_SLOTS[g]):
                for j in proj_jobs(c0, w):
                    n = plan.proj_no[L, g, s, j]
                    act.wait_ge(sem("jobs_done"), plan.job_no[L, g, s, j])
                    if isinstance(j, tuple):
                        f, st = j
                        f += (c0 - GDF0) // P
                        dst, src = (FM[:, f, 1:1 + CTX], ps(n % 2, CTX)) if st == 0 else (FM[:, f, 3 + CTX:3 + TOK], ps(n % 2, SEQ))
                    else:
                        dst, src = dest[:, j, c0 - base:c0 - base + w], ps(n % 2, w)
                    if g == "at":
                        nc.scalar.activation(P3[:, j, 0:256].rearrange("p (b a c) -> p a b c", b=2, a=2),
                                             ps(n % 2, 256).rearrange("p (a b c) -> p a b c", a=2, b=2), ACT.Copy)
                        dst, src = P3[:, j, 256:512], psum[:, n % 2, 256:512]
                    nc.scalar.activation(dst, src, ACT.Copy).then_inc(sem("proj_evac"), 1)
                    if isinstance(j, tuple) and st == 1 and f >= 1:
                        gd_conv_act(act, L, f - 1)
                if g == "gd" and s == 0:
                    gd_gates_act(act, L)
            if g == "gd":
                gd_conv_act(act, L, 5)

        def rope_pool(pool, view, nh, i, t4):
            x = view.rearrange("p (a b c) -> p a b c", b=2, c=16)
            t = [t4[:, 32 * nh * q:32 * nh * (q + 1)].rearrange("p (a c) -> p a c", c=16) for q in range(4)]
            cs = [bc_mid(tab(n)[:, 32 * (i - CT):32 * (i - CT) + 32], nh).rearrange("p h (a c) -> p h a c", a=2) for n in ("cos", "sin")]
            x1, x2 = x[:, :, 0, :], x[:, :, 1, :]
            hv = lambda v: v.rearrange("p (h a) c -> p h a c", a=2)
            nc.gpsimd.tensor_tensor(hv(t[0]), hv(x1), cs[0], ALU.mult)
            nc.gpsimd.tensor_tensor(hv(t[1]), hv(x2), cs[1], ALU.mult)
            nc.gpsimd.tensor_tensor(hv(t[2]), hv(x2), cs[0], ALU.mult)
            pchain(nc.gpsimd.tensor_tensor(hv(t[3]), hv(x1), cs[1], ALU.mult))
            nc.gpsimd.tensor_tensor(x1, t[0], t[1], ALU.subtract)
            return nc.gpsimd.tensor_tensor(x2, t[2], t[3], ALU.add)

        KDEC = regQ[:, :].rearrange("p (t d c) -> p t d c", t=NT, d=2)
        r_qk = [T[:, 512 * b:512 * b + 512] for b in range(2)]
        r_pm = [T[:, 1024 + 512 * b:1536 + 512 * b] for b in range(2)]
        r_tmp = regA[:, 6144:7168]

        def ret_pool(pool, L):
            pool.wait_ge(sem("proj_evac"), plan.proj_end[L, "ret"])
            for i in range(CT, NT):
                ins = rope_pool(pool, P1[:, i, 0:512], 8, i, r_tmp)
                if i < NT - 1:
                    pchain(ins)
            ins.then_inc(sem("ret_roped"), 1)

        def ret_dve(dve, L):
            dve.wait_ge(sem("proj_evac"), plan.proj_end[L, "ret"])
            dve.wait_ge(sem("ret_roped"), before(L, "ret_roped") + 1)
            for d in range(2):
                for i in range(NT):
                    kd = tab("ret_kdec")[:, 4 * d:4 * d + 4]
                    ins = nc.vector.tensor_tensor(heads(KDEC[:, i, d, :]), heads(P1[:, i, 256:512]), bc_in(kd, HD), ALU.mult)
            ins.then_inc(sem("ret_kdec"), 1)
            dve.wait_ge(sem("ret_kdec"), before(L, "ret_kdec") + 1)
            for i in range(NT):
                dve.wait_ge(sem("ret_turn_evac"), before(L, "ret_turn_evac") + i + 1)
                for d in range(2):
                    ins = nc.vector.tensor_tensor(QX_of["ret"][:, i, d, :], r_qk[i % 2][:, 0:256],
                                                  tab("ret_qdec")[:, 256 * d:256 * d + 256], ALU.mult)
                ins.then_inc(sem("ret_qx"), 1)
                dve.wait_ge(sem("ret_scores"), before(L, "ret_scores") + i + 1)
                if i >= 2:
                    dve.wait_ge(sem("ret_own"), before(L, "ret_own") + i - 1)
                nc.vector.tensor_tensor(r_pm[i % 2].rearrange("p (a c) -> p a c", a=2), psum[:, 4:6, 0:256],
                                        tab("ret_decay").rearrange("p (a c) -> p a c", a=2), ALU.mult).then_inc(sem("ret_pm"), 1)

        def ret_act(act, L):
            def own(i):
                act.wait_ge(sem("ret_own"), before(L, "ret_own") + i + 1)
                nc.scalar.activation(O_of["ret"][:, i, :], ps(6, 256), ACT.Copy)
                nc.scalar.activation(DS[:, i, :, :], ps(7, 256).rearrange("p (d c) -> p d c", d=2), ACT.Copy).then_inc(sem("ret_own_evac"), 1)
            for i in range(NT):
                act.wait_ge(sem("ret_turn"), before(L, "ret_turn") + i + 1)
                if i >= 2:
                    act.wait_ge(sem("ret_qx"), before(L, "ret_qx") + i - 1)
                    act.wait_ge(sem("ret_scores"), before(L, "ret_scores") + i - 1)
                nc.scalar.activation(r_qk[i % 2], ps(2 + i % 2), ACT.Copy).then_inc(sem("ret_turn_evac"), 1)
                if i >= 1:
                    own(i - 1)
            own(NT - 1)

        def ret_pe(pe, L):
            def own(i):
                pe.wait_ge(sem("ret_pm"), before(L, "ret_pm") + i + 1)
                if i >= 1:
                    pe.wait_ge(sem("ret_own_evac"), before(L, "ret_own_evac") + i)
                for h in range(HEADS):
                    nc.tensor.matmul(psum[:, 6, HD * h:HD * h + HD], r_pm[i % 2][:, P * hpos(h):P * hpos(h) + P],
                                     P1[:, i, 512 + HD * h:512 + HD * h + HD], start=True, stop=True)
                ins = own_state(i, 7, 0, lambda d, h: KDEC[:, i, d, HD * h:HD * h + HD],
                                lambda h: P1[:, i, 512 + HD * h:512 + HD * h + HD])
                ins.then_inc(sem("ret_own"), 1)

            pe.wait_ge(sem("ret_kdec"), before(L, "ret_kdec") + 1)
            for i in range(NT + 1):
                if i < NT:
                    if i >= 2:
                        pe.wait_ge(sem("ret_turn_evac"), before(L, "ret_turn_evac") + i - 1)
                    for b in range(4):
                        ins = nc.tensor.transpose(psum[:, 2 + i % 2, P * b:P * b + P], P1[:, i, P * b:P * b + P], ident)
                    ins.then_inc(sem("ret_turn"), 1)
                    pe.wait_ge(sem("ret_turn_evac"), before(L, "ret_turn_evac") + i + 1)
                    if i >= 1:
                        pe.wait_ge(sem("ret_pm"), before(L, "ret_pm") + i)
                    for h in range(HEADS):
                        q = r_qk[i % 2][half_of(h), P * (h // 2):P * (h // 2) + P]
                        k = r_qk[i % 2][half_of(h), 256 + P * (h // 2):256 + P * (h // 2) + P]
                        ins = nc.tensor.matmul(psum[:, 4 + h % 2, P * (h // 2):P * (h // 2) + P], k, q, start=True, stop=True)
                    ins.then_inc(sem("ret_scores"), 1)
                if i >= 1:
                    own(i - 1)

        def own_state(i, bank, col, key, val, dirs=(0, 1)):
            for d in dirs:
                for h in range(HEADS):
                    c = col + P * d + HD * (h // 2)
                    ins = nc.tensor.matmul(psum[half_of(h), bank, c:c + HD], key(d, h), val(h), start=True, stop=True)
            return ins

        def scan_dve(dve, L, g, last_own):
            dve.wait_ge(*last_own)
            for step in range(1, NT):
                for d in range(2):
                    a, b = ORDERS[d][step - 1], ORDERS[d][step]
                    for pair in range(2):
                        cols = slice(HD * pair, HD * pair + HD)
                        dec = tab("ret_cdec")[:, 2 * d + pair:2 * d + pair + 1] if g == "ret" else DEC[:, a, d, pair:pair + 1]
                        if step == 1:
                            ins = nc.vector.tensor_copy(SST[:, b, d, cols], DS[:, a, d, cols])
                        else:
                            ins = nc.vector.scalar_tensor_tensor(out=SST[:, b, d, cols], in0=SST[:, a, d, cols], scalar=dec,
                                                                 in1=DS[:, a, d, cols], op0=ALU.mult, op1=ALU.add)
                dchain(ins)
            nc.vector.memset(stat[:, 63:64], 0.0).then_inc(sem("scanned"), 1)

        def end_pe(pe, L, g):
            pe.wait_ge(sem("scanned"), ended("scanned", L, g) + 1)
            tiles = out_tiles(L)
            for n, i in enumerate(tiles):
                if n >= 2:
                    pe.wait_ge(sem("osum"), ended("osum", L, g) + n - 1)
                dirs = [d for d in range(2) if ORDERS[d][0] != i]
                for h in range(HEADS):
                    for d in dirs:
                        ins = nc.tensor.matmul(psum[:, (2, 6)[n % 2] + h % 2, HD * (h // 2):HD * (h // 2) + HD],
                                               QX_of[g][half_of(h), i, d, P * (h // 2):P * (h // 2) + P],
                                               SST[half_of(h), i, d, HD * (h // 2):HD * (h // 2) + HD],
                                               start=(d == dirs[0]), stop=(d == dirs[-1]))
                ins.then_inc(sem("inter"), 1)
            turn_y_pe(pe, L, g, lambda i, b: O_of[g][:, i, P * b:P * b + P])

        def turn_y_pe(pe, L, g, src):
            pe.wait_ge(sem("y"), ended("y", L, g) + 1)
            for n, i in enumerate(out_tiles(L)):
                if n >= 2:
                    pe.wait_ge(sem("yevac"), ended("yevac", L, g) + n - 1)
                for b in range(2):
                    ins = nc.tensor.transpose(psum[:, 4 + n % 2, P * b:P * b + P], src(i, b), ident)
                ins.then_inc(sem("yturn"), 1)

        def end_dve(dve, L, g):
            tiles = out_tiles(L)
            t0, nt = tiles[0], len(tiles)
            O, G = O_of[g], G_of[g]
            for n, i in enumerate(tiles):
                dve.wait_ge(sem("inter"), ended("inter", L, g) + n + 1)
                own = O[:, i, :].rearrange("p (a b c) -> p b a c", a=2, b=2)
                b0 = (2, 6)[n % 2]
                nc.vector.tensor_tensor(own, own, psum[:, b0:b0 + 2, 0:P].rearrange("p b (a c) -> p b a c", a=2),
                                        ALU.add).then_inc(sem("osum"), 1)
            dve.wait_ge(sem("osum"), ended("osum", L, g) + nt)
            w = nt * 256
            sq, ex = C0[:, 0:w], C1[:, 0:w]
            dve.wait_ge(sem("sq"), ended("sq", L, g) + 1)
            nc.vector.tensor_reduce(small[:, 64:64 + 4 * nt], sq.rearrange("p (a c) -> p a c", c=HD), AX.X, ALU.add).then_inc(sem("ss"), 1)
            ex3 = ex.rearrange("p (t c) -> p t c", t=nt)
            dchain(nc.vector.tensor_tensor(ex3, ex3, G[:, t0:, :], ALU.mult))
            gr = gains[:, GAIN[g], L, :]
            dchain(nc.vector.tensor_tensor(ex.rearrange("p (a c) -> p a c", c=HD), ex.rearrange("p (a c) -> p a c", c=HD), bc_mid(gr, 4 * nt), ALU.mult))
            dve.wait_ge(sem("rs"), ended("rs", L, g) + 1)
            dchain(nc.vector.tensor_tensor(ex.rearrange("p (a c) -> p a c", c=HD), ex.rearrange("p (a c) -> p a c", c=HD), bc_in(small[:, 128:128 + 4 * nt], HD), ALU.mult))
            nc.vector.tensor_tensor(O[:, t0:, :], O[:, t0:, :], ex3, ALU.mult).then_inc(sem("y"), 1)

        def end_act(act, L, g):
            tiles = out_tiles(L)
            t0, nt = tiles[0], len(tiles)
            O, G = O_of[g], G_of[g]
            w = nt * 256
            act.wait_ge(sem("osum"), ended("osum", L, g) + nt)
            nc.scalar.activation(C1[:, 0:w].rearrange("p (t c) -> p t c", t=nt), G[:, t0:, :], ACT.Sigmoid)
            nc.scalar.activation(C0[:, 0:w].rearrange("p (t c) -> p t c", t=nt), O[:, t0:, :], ACT.Square).then_inc(sem("sq"), 1)
            act.wait_ge(sem("ss"), ended("ss", L, g) + 1)
            achain(nc.scalar.activation(small[:, 96:96 + 4 * nt], small[:, 64:64 + 4 * nt], ACT.Ln, bias=eps_col, scale=1.0 / HD))
            nc.scalar.activation(small[:, 128:128 + 4 * nt], small[:, 96:96 + 4 * nt], ACT.Exp, scale=-0.5).then_inc(sem("rs"), 1)
            evac_y_act(act, L, g)

        def evac_y_act(act, L, g):
            tiles = out_tiles(L)
            for n, i in enumerate(tiles):
                act.wait_ge(sem("yturn"), ended("yturn", L, g) + n + 1)
                ins = nc.scalar.activation(yT[:, 2 * BR[g]:2 * BR[g] + 2, tok_tile(i)], heads(ps(4 + n % 2, 256), 2), ACT.Copy)
                if n < len(tiles) - 1:
                    ins.then_inc(sem("yevac"), 1)
            ins.then_inc(sem("yT"), 1)

        HQ = P2[:, :, 0:256]
        HZ = P2[:, :, 256:768]
        KK = regQ[:, :].rearrange("p (t c) -> p t c", t=NT)
        h_qk = [regA[:, 3072 + 768 * b:3840 + 768 * b] for b in range(2)]
        h_ee = [regA[:, 4608 + 1024 * b:5632 + 1024 * b].rearrange("p (a c) -> p a c", a=2) for b in range(2)]
        h_en = [regA[:, 6656 + 256 * b:6912 + 256 * b].rearrange("p (a c) -> p a c", a=2) for b in range(2)]
        h_eb = regA[:, 7168:7680]
        h_pm = [T[:, 512 * b:512 * b + 512] for b in range(2)]
        h_mc = [T[:, 1024 + 256 * b:1280 + 256 * b].rearrange("p (a c) -> p a c", a=2) for b in range(2)]
        zeros = T[:, 1536:1664].bitcast(BF16)
        CLAMP = 80.0
        ZMIN = -40.0

        def hg_bounds(L):
            return C1[:, 0:512], C1[:, 512:1024]

        def hg_pool(pool, L):
            pool.wait_ge(sem("yT"), ended("yT", L, "ret") + 1)
            nc.gpsimd.memset(zeros, 0.0).then_inc(sem("zeros_set"), 1)
            if L:
                for dep in range(2):
                    for d in range(2):
                        pool.dma_start(C1[:, 512 * dep + 256 * d:512 * dep + 256 * d + 256],
                                       A["hg_lb_logits"][d, dep].partition_broadcast(P)).then_inc(sem("logits_loaded"), 16)
            for n in range(2 * NT):
                i, d = divmod(n, 2)
                if d == 0:
                    pool.wait_ge(sem("hg_eb"), before(L, "hg_eb") + i + 1)
                    nc.gpsimd.tensor_tensor(h_eb, h_eb, KK[:, i, :], ALU.mult).then_inc(sem("hg_kb"), 1)
                pool.wait_ge(sem("hg_ee"), before(L, "hg_ee") + n + 1)
                e, qk = h_ee[n % 2], h_qk[i % 2]
                q, k = [qk[:, o:o + 256].rearrange("p (a c) -> p a c", a=2) for o in (0, 256 + 256 * d)]
                qs, ks = (slice(64, P), slice(0, 64)) if d == 0 else (slice(0, 64), slice(64, P))
                f0 = e[:, :, P:2 * P]
                nc.gpsimd.tensor_tensor(f0[:, :, qs], f0[:, :, qs], q[:, :, qs], ALU.mult)
                nc.gpsimd.tensor_tensor(f0[:, :, ks], f0[:, :, ks], k[:, :, ks], ALU.mult)
                blk = lambda v, side: v.rearrange("p a (b s c) -> p a b s c", b=2, s=2)[:, :, :, side, :]
                f1 = e[:, :, 2 * P:3 * P]
                nc.gpsimd.tensor_tensor(blk(f1, 1 - d), blk(f1, 1 - d), blk(q, 1 - d), ALU.mult)
                nc.gpsimd.tensor_tensor(blk(f1, d), blk(f1, d), blk(k, d), ALU.mult).then_inc(sem("hg_fac_pool"), 1)
                if d == 1:
                    pool.wait_ge(sem("hg_pm"), before(L, "hg_pm") + n + 1)
                    nc.gpsimd.tensor_tensor(h_pm[0], h_pm[0], h_pm[1], ALU.add).then_inc(sem("hg_pmsum"), 1)

        def hg_dve(dve, L):
            dve.wait_ge(sem("proj_evac"), plan.proj_end[L, "hg"])
            if L:
                dve.wait_ge(sem("logits_loaded"), 64)
                oml, lb = hg_bounds(L)
                dchain(nc.vector.tensor_tensor(oml, oml, lb, ALU.subtract))
                nc.vector.tensor_scalar(lb, oml, 1.0, None, ALU.mult).then_inc(sem("hg_bound"), 1)
            nc.vector.tensor_scalar(HZ, HZ, ZMIN, None, ALU.max).then_inc(sem("hg_z"), 1)
            if L:
                dve.wait_ge(sem("lb_exp"), 1)
                dchain(nc.vector.tensor_scalar(lb, lb, 1.0, None, ALU.add))
                dchain(nc.vector.reciprocal(lb, lb))
                dchain(nc.vector.tensor_scalar(oml, lb, -1.0, 1.0, ALU.mult, ALU.add))
            dve.wait_ge(sem("hg_sigmoids"), before(L, "hg_sigmoids") + 1)
            if L:
                dchain(nc.vector.tensor_tensor(HZ, HZ, bc_mid(oml, NT), ALU.mult))
                nc.vector.tensor_tensor(HZ, HZ, bc_mid(lb, NT), ALU.add).then_inc(sem("hg_bound"), 1)
                nc.vector.tensor_tensor(KK, KK, bc_mid(oml, NT), ALU.mult)
            nc.vector.tensor_tensor(HQ, HQ, C0.rearrange("p (t c) -> p t c", t=NT), ALU.mult).then_inc(sem("hg_q"), 1)

            def pm(n):
                dve.wait_ge(sem("hg_pt"), before(L, "hg_pt") + n + 1)
                if n >= 2 and n % 2 == 0:
                    dve.wait_ge(sem("hg_own"), before(L, "hg_own") + n // 2)
                nc.vector.tensor_tensor(h_pm[n % 2].rearrange("p (a b c) -> p a b c", a=2, b=2),
                                        psum[:, 6:8, 0:256].rearrange("p a (b c) -> p a b c", b=2),
                                        bc_mid(run[n % 2], 4).rearrange("p (a b) c -> p a b c", a=2), ALU.mult).then_inc(sem("hg_pm"), 1)

            for n in range(2 * NT):
                i, d = divmod(n, 2)
                if n == 5:
                    at_ss_dve(dve, L)
                elif n == 8:
                    at_norm_dve(dve, L)
                dve.wait_ge(sem("hg_sums"), before(L, "hg_sums") + n + 1)
                if n >= 2:
                    dve.wait_ge(sem("hg_ee"), before(L, "hg_ee") + n - 1)
                nc.vector.tensor_scalar(h_mc[n % 2], psum[:, 2:4, 3 * P:4 * P], CLAMP, -CLAMP, ALU.min, ALU.max).then_inc(sem("hg_mc"), 1)
                if n >= 1:
                    pm(n - 1)
                dve.wait_ge(sem("hg_ee"), before(L, "hg_ee") + n + 1)
                e, en, qk = h_ee[n % 2], h_en[n % 2], h_qk[i % 2]
                q, k = [qk[:, o:o + 256].rearrange("p (a c) -> p a c", a=2) for o in (0, 256 + 256 * d)]
                nc.vector.tensor_tensor(e[:, :, 3 * P:4 * P], e[:, :, 3 * P:4 * P], q, ALU.mult)
                nc.vector.tensor_tensor(en, en, k, ALU.mult).then_inc(sem("hg_fac_dve"), 1)
                last = P - 1 if d == 0 else 0
                nc.vector.tensor_copy(DEC[:, i, d, :], e[:, :, last:last + 1].rearrange("p a c -> p (a c)"))
                nc.vector.tensor_tensor(QX_of["hg"][:, i, d, :].rearrange("p (a c) -> p a c", a=2), e[:, :, 0:P], q, ALU.mult).then_inc(sem("hg_qx"), 1)
            pm(2 * NT - 1)
            dve.wait_ge(sem("hg_qx"), before(L, "hg_qx") + 2 * NT)

        def hg_act(act, L):
            if L:
                act.wait_ge(sem("hg_bound"), 1)
                _, lb = hg_bounds(L)
                nc.scalar.activation(lb, lb, ACT.Exp).then_inc(sem("lb_exp"), 1)
            act.wait_ge(sem("hg_z"), before(L, "hg_z") + 1)
            achain(nc.scalar.activation(KK, HZ, ACT.Sigmoid, scale=-1.0))
            nc.scalar.activation(HZ, HZ, ACT.Sigmoid)
            nc.scalar.activation(C0.rearrange("p (t c) -> p t c", t=NT), HQ, ACT.Sigmoid).then_inc(sem("hg_sigmoids"), 1)
            act.wait_ge(sem("hg_sigmoids"), L + 1)
            if L:
                act.wait_ge(sem("hg_bound"), 2)
            nc.scalar.activation(HZ, HZ, ACT.Ln).then_inc(sem("hg_lf"), 1)

            def own(i):
                act.wait_ge(sem("hg_own"), before(L, "hg_own") + i + 1)
                nc.scalar.activation(O_of["hg"][:, i, :], ps(4, 256), ACT.Copy)
                nc.scalar.activation(DS[:, i, :, :], psum[:, 4, 256:512].rearrange("p (d c) -> p d c", d=2), ACT.Copy).then_inc(sem("hg_own_evac"), 1)

            for n in range(2 * NT):
                i, d = divmod(n, 2)
                if n == 3:
                    at_square_act(act, L)
                elif n == 7:
                    at_rs_act(act, L)
                if d == 0:
                    if i >= 1:
                        own(i - 1)
                    act.wait_ge(sem("hg_tail"), before(L, "hg_tail") + i + 1)
                    nc.scalar.activation(h_eb, ps(4), ACT.Exp).then_inc(sem("hg_eb"), 1)
                    act.wait_ge(sem("hg_turn"), before(L, "hg_turn") + i + 1)
                    if i >= 2:
                        act.wait_ge(sem("hg_qx"), before(L, "hg_qx") + 2 * (i - 1))
                        act.wait_ge(sem("hg_fac_pool"), before(L, "hg_fac_pool") + 2 * (i - 1))
                    nc.scalar.activation(h_qk[i % 2][:, 0:512], ps(5), ACT.Copy)
                    nc.scalar.activation(h_qk[i % 2][:, 512:768], ps(6, 256), ACT.Copy).then_inc(sem("hg_turn_evac"), 1)
                act.wait_ge(sem("hg_sums"), before(L, "hg_sums") + n + 1)
                if n >= 2:
                    act.wait_ge(sem("hg_pt"), before(L, "hg_pt") + n - 1)
                    act.wait_ge(sem("hg_qx"), before(L, "hg_qx") + n - 1)
                e, en = h_ee[n % 2], h_en[n % 2]
                act.wait_ge(sem("hg_mc"), before(L, "hg_mc") + n + 1)
                nc.scalar.activation(e[:, :, 0:3 * P], psum[:, 2:4, 0:3 * P], ACT.Exp)
                nc.scalar.activation(e[:, :, 3 * P:4 * P], h_mc[n % 2], ACT.Exp)
                nc.scalar.activation(en, h_mc[n % 2], ACT.Exp, scale=-1.0).then_inc(sem("hg_ee"), 1)
            own(NT - 1)

        def hg_pe(pe, L):
            pe.wait_ge(sem("hg_lf"), before(L, "hg_lf") + 1)
            pe.wait_ge(sem("hg_q"), before(L, "hg_q") + 1)
            pe.wait_ge(sem("zeros_set"), L + 1)

            def sums_of(n):
                i, d = divmod(n, 2)
                if n >= 1:
                    pe.wait_ge(sem("hg_ee"), before(L, "hg_ee") + n)
                for pair in range(2):
                    ins = nc.tensor.matmul(ps(2 + pair), HZ[:, i, 256 * d + P * pair:256 * d + P * pair + P], sums[d], start=True, stop=True)
                ins.then_inc(sem("hg_sums"), 1)

            def tail_and_turn(i):
                if i >= 1:
                    pe.wait_ge(sem("hg_own_evac"), before(L, "hg_own_evac") + i)
                for d in range(2):
                    ins = nc.tensor.matmul(psum[:, 4, 256 * d:256 * d + 256], tail[d], HZ[:, i, 256 * d:256 * d + 256], start=True, stop=True)
                ins.then_inc(sem("hg_tail"), 1)
                if i >= 1:
                    pe.wait_ge(sem("hg_turn_evac"), before(L, "hg_turn_evac") + i)
                    pe.wait_ge(sem("hg_pm"), before(L, "hg_pm") + 2 * i)
                for b in range(6):
                    src = P2[:, i, P * b:P * b + P] if b < 2 else KK[:, i, P * (b - 2):P * (b - 2) + P]
                    ins = nc.tensor.transpose(psum[:, 5 + b // 4, P * (b % 4):P * (b % 4) + P], src, ident)
                ins.then_inc(sem("hg_turn"), 1)

            def score(n):
                i, d = divmod(n, 2)
                pe.wait_ge(sem("hg_fac_dve"), before(L, "hg_fac_dve") + n + 1)
                pe.wait_ge(sem("hg_fac_pool"), before(L, "hg_fac_pool") + n + 1)
                pe.wait_ge(sem("hg_turn_evac"), before(L, "hg_turn_evac") + i + 1)
                if n >= 1:
                    pe.wait_ge(sem("hg_pm"), before(L, "hg_pm") + n)
                for hf in range(2):
                    nc.tensor.matmul(psum[:, 6 + hf, 0:256], zeros[:, 0:P], zeros, start=True, stop=False, skip_group_check=True)
                for h in range(HEADS):
                    hf, pr = h % 2, h // 2
                    rows = half_of(h)
                    e, en = h_ee[n % 2][rows, pr, :], h_en[n % 2][rows, pr, :]

                    def piece(s0, t0, size, k, q):
                        return nc.tensor.matmul(psum[s0:s0 + size, 6 + hf, P * pr + t0:P * pr + t0 + size], k, q,
                                                start=False, stop=True, skip_group_check=True)
                    for lev, size in ((1, 64), (2, 32)):
                        for b in range(64 // size):
                            o = 2 * size * b
                            s0, t0 = (o, o + size) if d == 0 else (o + size, o)
                            piece(s0, t0, size, e[:, P * lev + s0:P * lev + s0 + size], e[:, P * lev + t0:P * lev + t0 + size])
                    for b in range(4):
                        ins = piece(32 * b, 32 * b, 32, en[:, 32 * b:32 * b + 32], e[:, 3 * P + 32 * b:3 * P + 32 * b + 32])
                ins.then_inc(sem("hg_pt"), 1)

            def own(i):
                pe.wait_ge(sem("hg_pmsum"), before(L, "hg_pmsum") + i + 1)
                pe.wait_ge(sem("hg_kb"), before(L, "hg_kb") + i + 1)
                val = lambda h: P2[:, i, 768 + HD * h:768 + HD * h + HD]
                for h in range(HEADS):
                    nc.tensor.matmul(psum[:, 4, HD * h:HD * h + HD], h_pm[0][:, P * hpos(h):P * hpos(h) + P], val(h), start=True, stop=True)
                own_state(i, 4, 256, lambda d, h: h_eb[:, 256 * d + HD * h:256 * d + HD * h + HD], val).then_inc(sem("hg_own"), 1)

            for n in range(2 * NT + 1):
                if n < 2 * NT:
                    sums_of(n)
                if n >= 1:
                    score(n - 1)
                    if n % 2 == 0:
                        own(n // 2 - 1)
                if n < 2 * NT and n % 2 == 0:
                    tail_and_turn(n // 2)

        QT = regQ[:, 0:1536].rearrange("p (b t) -> p b t", b=2)
        KT = regQ[:, 1536:2304]
        a_px = [regA[:, 3072 + 768 * b:3840 + 768 * b] for b in range(2)]
        a_pt = [regA[:, 4608 + 768 * b:5376 + 768 * b] for b in range(2)]
        A_SS, A_LN, A_RS, A_MAX, A_SUM, A_INV = 256, 304, 352, 144, 152, 176
        A_TMP = yT[:, 4:8, :].rearrange("p b t -> p (b t)")

        def at_steps(L):
            return [(i, h) for i in out_tiles(L) for h in (0, 2, 1, 3)]

        def at_pool(pool, L):
            pool.wait_ge(sem("at_normed"), before(L, "at_normed") + 1)
            for i in range(CT, NT):
                ins = rope_pool(pool, P3[:, i, 0:384], 6, i, A_TMP[:, 2304:3072])
                if i < NT - 1:
                    pchain(ins)
            ins.then_inc(sem("at_roped"), 1)

        def at_ss_dve(dve, L):
            dve.wait_ge(sem("at_sq"), before(L, "at_sq") + 1)
            nc.vector.tensor_reduce(small[:, A_SS:A_SS + 36], A_TMP[:, 0:2304].rearrange("p (a c) -> p a c", c=HD), AX.X, ALU.add).then_inc(sem("at_ss"), 1)

        def at_norm_dve(dve, L):
            qk = P3[:, :, 0:384].rearrange("p t (h c) -> p t h c", h=6)
            dve.wait_ge(sem("at_rs"), before(L, "at_rs") + 1)
            rs = small[:, A_RS:A_RS + 36].rearrange("p (t h) -> p t h", t=NT).unsqueeze(3).to_broadcast([P, NT, 6, HD])
            dchain(nc.vector.tensor_tensor(qk, qk, rs, ALU.mult))
            for o, n, g in ((0, 4, 3), (4, 2, 4)):
                gn = gains[:, g, L, :].unsqueeze(1).unsqueeze(1).to_broadcast([P, NT, n, HD])
                ins = nc.vector.tensor_tensor(qk[:, :, o:o + n, :], qk[:, :, o:o + n, :], gn, ALU.mult)
            ins.then_inc(sem("at_normed"), 1)

        def at_dve(dve, L):
            steps = at_steps(L)

            def probs_t(m):
                i, h = steps[m]
                w = CTX if i < CT else TOK
                dve.wait_ge(sem("at_pturn"), before(L, "at_pturn") + m + 1)
                if m >= 2:
                    dve.wait_ge(sem("at_pv"), before(L, "at_pv") + m - 1)
                nc.vector.tensor_copy(a_pt[m % 2][:, 0:w], psum[:, 6:8, :].rearrange("p b c -> p (b c)")[:, 0:w]).then_inc(sem("at_pt"), 1)

            def finish(m):
                i = steps[m][0]
                dve.wait_ge(sem("at_pv"), before(L, "at_pv") + m + 1)
                dchain(nc.vector.reciprocal(small[:, A_INV + 4 * i:A_INV + 4 * i + 4], small[:, A_SUM + 4 * i:A_SUM + 4 * i + 4]))
                ins = nc.vector.tensor_tensor(heads(P3[:, i, 0:256]), heads(ps(i % 2, 256)),
                                              bc_in(small[:, A_INV + 4 * i:A_INV + 4 * i + 4], HD), ALU.mult)
                ins.then_inc(sem("at_ytile"), 1)

            for m in range(len(steps) + 2):
                if m < len(steps):
                    i, h = steps[m]
                    w = CTX if i < CT else TOK
                    b = 2 + 2 * (m % 2)
                    mx = small[:, A_MAX + m % 4:A_MAX + m % 4 + 1]
                    dve.wait_ge(sem("at_scores"), before(L, "at_scores") + m + 1)
                    if m >= 4:
                        dve.wait_ge(sem("at_exp"), before(L, "at_exp") + m - 3)
                    dchain(nc.vector.tensor_reduce(mx, psum[:, b:b + 2, :].rearrange("p b c -> p (b c)")[:, 0:w], AX.X, ALU.max, negate=True))
                    nc.vector.tensor_scalar(mx, mx, QSCALE, None, ALU.mult).then_inc(sem("at_max"), 1)
                if 1 <= m <= len(steps):
                    probs_t(m - 1)
                if m >= 2 and (m - 2) % 4 == 3:
                    finish(m - 2)
            dve.wait_ge(sem("at_ytile"), before(L, "at_ytile") + len(out_tiles(L)))
            nc.vector.memset(stat[:, 61:62], 0.0).then_inc(sem("y"), 1)

        def at_square_act(act, L):
            act.wait_ge(sem("proj_evac"), plan.proj_end[L, "at"])
            nc.scalar.activation(A_TMP[:, 0:2304].rearrange("p (t c) -> p t c", t=NT), P3[:, :, 0:384], ACT.Square).then_inc(sem("at_sq"), 1)

        def at_rs_act(act, L):
            act.wait_ge(sem("at_ss"), before(L, "at_ss") + 1)
            achain(nc.scalar.activation(small[:, A_LN:A_LN + 36], small[:, A_SS:A_SS + 36], ACT.Ln, bias=eps_col, scale=1.0 / HD))
            nc.scalar.activation(small[:, A_RS:A_RS + 36], small[:, A_LN:A_LN + 36], ACT.Exp, scale=-0.5).then_inc(sem("at_rs"), 1)

        def at_act(act, L):
            for i in range(NT):
                act.wait_ge(sem("at_turn"), before(L, "at_turn") + i + 1)
                nc.scalar.activation(QT[:, :, tok_tile(i)], heads(ps(2 + i % 2, 256), 2), ACT.Copy)
                nc.scalar.activation(KT[:, tok_tile(i)], psum[:, 2 + i % 2, 256:384], ACT.Copy).then_inc(sem("at_turn_evac"), 1)
            for m, (i, h) in enumerate(at_steps(L)):
                w = CTX if i < CT else TOK
                b = 2 + 2 * (m % 2)
                act.wait_ge(sem("at_max"), before(L, "at_max") + m + 1)
                if m >= 2:
                    act.wait_ge(sem("at_pturn"), before(L, "at_pturn") + m - 1)
                nc.scalar.activation(a_px[m % 2][:, 0:w], psum[:, b:b + 2, :].rearrange("p b c -> p (b c)")[:, 0:w], ACT.Exp,
                                     bias=small[:, A_MAX + m % 4:A_MAX + m % 4 + 1], scale=QSCALE,
                                     accum_out=small[:, A_SUM + 4 * i + h:A_SUM + 4 * i + h + 1]).then_inc(sem("at_exp"), 1)
            evac_y_act(act, L, "at")

        def at_pe(pe, L):
            pe.wait_ge(sem("at_roped"), before(L, "at_roped") + 1)
            for i in range(NT):
                if i >= 2:
                    pe.wait_ge(sem("at_turn_evac"), before(L, "at_turn_evac") + i - 1)
                for b in range(2):
                    nc.tensor.transpose(psum[:, 2 + i % 2, P * b:P * b + P], P3[:, i, P * b:P * b + P], ident)
                ins = nc.tensor.transpose(psum[:, 2 + i % 2, 256:384], P3[:, i, 256:384], ident)
                ins.then_inc(sem("at_turn"), 1)
            pe.wait_ge(sem("at_turn_evac"), before(L, "at_turn_evac") + NT)
            pe.wait_ge(sem("proj_evac"), plan.proj_end[L, "at"])
            steps = at_steps(L)
            for m in range(len(steps) + 2):
                if m < len(steps):
                    i, h = steps[m]
                    rows, b = slice(64 * (h // 2), 64 * (h // 2) + 64), 2 + 2 * (m % 2)
                    if m >= 2:
                        pe.wait_ge(sem("at_exp"), before(L, "at_exp") + m - 1)
                    for k0, k1 in (((0, CTX),) if i < CT else ((0, 512), (512, TOK))):
                        ins = nc.tensor.matmul(psum[:, b + k0 // 512, 0:k1 - k0], QT[rows, h % 2, tok_tile(i)], KT[rows, k0:k1], start=True, stop=True)
                    ins.then_inc(sem("at_scores"), 1)
                if 1 <= m <= len(steps):
                    i, h = steps[m - 1]
                    pe.wait_ge(sem("at_exp"), before(L, "at_exp") + m)
                    if m >= 2:
                        pe.wait_ge(sem("at_pt"), before(L, "at_pt") + m - 1)
                    for c in range(CT if i < CT else NT):
                        ins = nc.tensor.transpose(psum[:, 6 + c // 4, P * (c % 4):P * (c % 4) + P], a_px[(m - 1) % 2][:, P * c:P * c + P], ident)
                    ins.then_inc(sem("at_pturn"), 1)
                if m >= 2:
                    i, h = steps[m - 2]
                    pe.wait_ge(sem("at_pt"), before(L, "at_pt") + m - 1)
                    t = out_tiles(L).index(i)
                    if t >= 2:
                        pe.wait_ge(sem("at_ytile"), before(L, "at_ytile") + t - 1)
                    nk = CT if i < CT else NT
                    for c in range(nk):
                        ins = nc.tensor.matmul(psum[:, i % 2, HD * h:HD * h + HD], a_pt[(m - 2) % 2][:, P * c:P * c + P],
                                               P3[:, c, 384 + HD * (h // 2):384 + HD * (h // 2) + HD], start=(c == 0), stop=(c == nk - 1))
                    ins.then_inc(sem("at_pv"), 1)
            turn_y_pe(pe, L, "at", lambda i, b: P3[:, i, P * b:P * b + P])

        GB = regB[:, 3072:7680]
        g_buf = lambda j: GB[:, 512 * j:512 * j + 512] if j < 9 else C1[:, 512 * (j - 9):512 * (j - 9) + 512]
        g_gm, g_pm, g_am, g_t, g_u, g_x = [[g_buf(6 * d + j) for d in range(2)] for j in range(6)]
        g_r = T[:, 0:1024].rearrange("p (d c) -> p d c", d=2)
        g_qt = T[:, 1024:1536].rearrange("p (d c) -> p d c", d=2)
        g_kt = T[:, 1536:2048].rearrange("p (d c) -> p d c", d=2)
        g_qkn, g_qkT, g_v = regA[:, 6264:6776], regA[:, 6776:7288], regA[:, 7288:7544]
        g_cv = [T[:, 772 * b:772 * b + 770] for b in range(2)]
        g_ev = [GB[:, 772 * b:772 * b + 770] for b in range(2)]
        tab48 = lambda o: small[:, o:o + 48].rearrange("p (t c) -> p t c", t=NT)
        g_gate, g_beta, g_nbeta, g_t1, g_t2 = tab48(128), tab48(176), tab48(224), tab48(416), tab48(464)
        g_eg = small[:, 272:416]
        g_cum = [small[:, 272 + 24 * d:296 + 24 * d].rearrange("p (t h) -> p t h", t=NT) for d in range(2)]
        g_tail = [small[:, 320 + 24 * d:344 + 24 * d].rearrange("p (t h) -> p t h", t=NT) for d in range(2)]
        g_tot = small[:, 368:416].rearrange("p (t c) -> p t c", t=NT)
        nea = stat[:, 32:40]
        MERGES = 7
        tile_cols = lambda i: slice(1 + P * i, 1 + P * i + P) if i < CT else slice(3 + P * i, 3 + P * i + P)

        def by_pos(ap):
            return ap.rearrange("p (a b) -> p b a", b=2)

        def sq4(ap):
            return ap.rearrange("p (a b c) -> p a b c", a=2, b=2)

        mmask = yT[:, 2 * BR["gd"]:2 * BR["gd"] + 2, :].rearrange("p b t -> p (b t)")[:, 0:MERGES * P]

        def gd_pool(pool, L):
            pool.wait_ge(sem("yT"), ended("yT", L, "at") + 1)
            pool.dma_start(mmask.bitcast(U16), masks).then_inc(sem("masks_loaded"), 16)
            for c in (0, CTX + 1, CTX + 2, CHP - 1):
                ins = nc.gpsimd.memset(FM[:, :, c:c + 1], 0.0)
            ins.then_inc(sem("gd_pads"), 1)
            am = 0
            for i in range(NT):
                pool.wait_ge(sem("gd_cum"), before(L, "gd_cum") + 1)
                pool.wait_ge(sem("gd_conv"), before(L, "gd_conv") + 1)
                if i >= 1:
                    pool.wait_ge(sem("gd_am"), before(L, "gd_am") + 2 * MERGES * i)
                for d in range(2):
                    g = by_pos(g_gate[:, i, 4 * d:4 * d + 4])
                    nc.gpsimd.tensor_tensor(sq4(g_gm[d]), bc_mid(run[d], 4).rearrange("p (a b) c -> p a b c", a=2),
                                            g.unsqueeze(3).to_broadcast([P, 2, 2, P]), ALU.mult).then_inc(sem("gd_ga"), 1)
                pool.wait_ge(sem("gd_qkn"), before(L, "gd_qkn") + i + 1)
                if i >= 1:
                    pool.wait_ge(sem("gd_fin"), before(L, "gd_fin") + 2 * i)
                for d in range(2):
                    r = g_r[:, d, :].rearrange("p (h c) -> p h c", h=HEADS)
                    k4, q4 = heads(g_qkn[:, 256:512]), heads(g_qkn[:, 0:256])
                    nc.gpsimd.tensor_tensor(heads(g_qt[:, d, :]), q4, bc_in(g_cum[d][:, i, :], HD), ALU.mult)
                    nc.gpsimd.tensor_tensor(heads(g_kt[:, d, :]), k4, bc_in(g_tail[d][:, i, :], HD), ALU.mult)
                    nc.gpsimd.tensor_tensor(r[:, :, HD:P], k4, bc_in(g_cum[d][:, i, :], HD), ALU.mult)
                    ins = nc.gpsimd.tensor_copy(r[:, :, 0:HD], heads(g_v))
                ins.then_inc(sem("gd_tiled"), 1)
                for m in range(MERGES):
                    for d in range(2):
                        if m == 0:
                            pool.wait_ge(sem("gd_at"), before(L, "gd_at") + 2 * i + d + 1)
                            b = by_pos(g_beta[:, i, 4 * d:4 * d + 4]).unsqueeze(3).to_broadcast([P, 2, 2, P])
                            pchain(nc.gpsimd.tensor_tensor(sq4(g_gm[d]), sq4(g_gm[d]), b, ALU.mult))
                        else:
                            pool.wait_ge(sem("gd_x"), before(L, "gd_x") + 2 * (MERGES * i + m - 1) + d + 1)
                            if m == 1:
                                pool.wait_ge(sem("gd_tu"), before(L, "gd_tu") + 2 * ((MERGES - 1) * i) + d + 1)
                        if i == m == d == 0:
                            pool.wait_ge(sem("masks_loaded"), 16 * (L + 1))
                        mk = mmask.bitcast(BF16)[:, P * (MERGES * d + m):P * (MERGES * d + m) + P]
                        nc.gpsimd.tensor_tensor(heads(g_am[d]), heads(g_gm[d]), bc_mid(mk, 4), ALU.mult).then_inc(sem("gd_am"), 1)
                    if m == 1:
                        for d in range(2):
                            nc.gpsimd.tensor_tensor(heads(g_pm[d]), heads(g_pm[d]), bc_mid(run[d], 4), ALU.mult).then_inc(sem("gd_pmm"), 1)

        def gd_dve(dve, L):
            dve.wait_ge(sem("proj_evac"), plan.proj_no[L, "gd", 0, NT - 1] + 1)
            dve.wait_ge(sem("gd_nea_exp"), before(L, "gd_nea_exp") + 1)
            dchain(nc.vector.tensor_scalar(nea, nea, -1.0, None, ALU.mult))
            dchain(nc.vector.tensor_tensor(g_t1, P4[:, :, 0:8], bc_mid(dtb[:, L, :], NT), ALU.add))
            dchain(nc.vector.tensor_scalar(g_t2, g_t1, -1.0, None, ALU.mult))
            nc.vector.tensor_tensor(g_t2, g_t2, g_t1, ALU.max).then_inc(sem("gd_abs"), 1)
            dve.wait_ge(sem("gd_sp"), before(L, "gd_sp") + 1)
            dchain(nc.vector.tensor_scalar(g_t1, g_t1, 0.0, None, ALU.max))
            dchain(nc.vector.tensor_tensor(g_t1, g_t1, g_t2, ALU.add))
            nc.vector.tensor_tensor(g_gate, g_t1, bc_mid(nea, NT), ALU.mult).then_inc(sem("gd_gate"), 1)
            dchain(nc.vector.tensor_scalar(g_nbeta, g_beta, -1.0, None, ALU.mult))
            dve.wait_ge(sem("gd_pads"), before(L, "gd_pads") + 1)

            def silu(f):
                dve.wait_ge(sem("gd_cve"), before(L, "gd_cve") + f + 1)
                nc.vector.tensor_tensor(FM[:, f, 1:771], g_cv[f % 2], g_ev[f % 2], ALU.mult).then_inc(sem("gd_silu"), 1)

            for f in range(6):
                slot, block = (1, f) if f < 4 else (2, f - 4)
                dve.wait_ge(sem("proj_evac"), plan.proj_no[L, "gd", slot, (block, 1)] + 1)
                x, w = FM[:, f, :], convT[:, L, :, f:f + 1]
                cv = g_cv[f % 2]
                if f >= 2:
                    dve.wait_ge(sem("gd_silu"), before(L, "gd_silu") + f - 1)
                dchain(nc.vector.tensor_scalar(cv, x[:, 1:771], w[:, 1], None, ALU.mult))
                dchain(nc.vector.scalar_tensor_tensor(out=cv, in0=x[:, 0:770], scalar=w[:, 0], in1=cv, op0=ALU.mult, op1=ALU.add))
                nc.vector.scalar_tensor_tensor(out=cv, in0=x[:, 2:772], scalar=w[:, 2], in1=cv, op0=ALU.mult, op1=ALU.add).then_inc(sem("gd_cv"), 1)
                if f >= 1:
                    silu(f - 1)
            silu(5)
            dve.wait_ge(sem("gd_silu"), before(L, "gd_silu") + 6)
            nc.vector.memset(stat[:, 60:61], 0.0).then_inc(sem("gd_conv"), 1)

            def finish(i, d):
                n = 2 * i + d
                dve.wait_ge(sem("gd_fin"), before(L, "gd_fin") + n + 1)
                O = O_of["gd"][:, i, :]
                if d == 0:
                    dchain(nc.vector.tensor_copy(O, psum[:, 4, 0:256]))
                else:
                    nc.vector.tensor_tensor(O, O, psum[:, 5, 0:256], ALU.add)
                for h in range(HEADS):
                    rows, c = half_of(h), slice(HD * (h // 2), HD * (h // 2) + HD)
                    ins = nc.vector.scalar_tensor_tensor(out=MT[rows, i, d, c], in0=tab("eye2")[rows, :], scalar=g_tot[rows, i, 4 * d + h:4 * d + h + 1],
                                                         in1=psum[rows, 4 + d, 384 + HD * (h // 2):448 + HD * (h // 2)], op0=ALU.mult, op1=ALU.add)
                ins.then_inc(sem("gd_evac_dve"), 1)

            for i in range(NT):
                dve.wait_ge(sem("gd_sq"), before(L, "gd_sq") + i + 1)
                nc.vector.tensor_reduce(small[:, 0:8], g_x[0].rearrange("p (a c) -> p a c", c=HD), AX.X, ALU.add).then_inc(sem("gd_ss"), 1)
                dve.wait_ge(sem("gd_rs"), before(L, "gd_rs") + i + 1)
                if i >= 1:
                    dve.wait_ge(sem("gd_tiled"), before(L, "gd_tiled") + i)
                dchain(nc.vector.tensor_scalar(small[:, 16:20], small[:, 16:20], QSCALE, None, ALU.mult))
                nc.vector.tensor_tensor(heads(g_qkn, 8), heads(ps(2), 8), bc_in(small[:, 16:24], HD), ALU.mult).then_inc(sem("gd_qkn"), 1)
                for d in range(2):
                    dve.wait_ge(sem("gd_gm"), before(L, "gd_gm") + 2 * i + d + 1)
                    if d == 0:
                        dve.wait_ge(sem("gd_scores"), before(L, "gd_scores") + i + 1)
                    nc.vector.tensor_tensor(sq4(g_pm[d]), psum[:, 4:6, 0:256].rearrange("p a (b c) -> p a b c", b=2), sq4(g_gm[d]), ALU.mult)
                    nc.vector.memset(stat[:, 59:60], 0.0).then_inc(sem("gd_pm"), 1)
                    dve.wait_ge(sem("gd_pm"), before(L, "gd_pm") + 2 * i + d + 1)
                    nc.vector.tensor_tensor(sq4(g_gm[d]), psum[:, 4:6, 256:512].rearrange("p a (b c) -> p a b c", b=2), sq4(g_gm[d]), ALU.mult).then_inc(sem("gd_at"), 1)
                for m in range(MERGES - 1):
                    for d in range(2):
                        if m == 0:
                            dve.wait_ge(sem("gd_x"), before(L, "gd_x") + 2 * MERGES * i + d + 1)
                            dve.wait_ge(sem("gd_am"), before(L, "gd_am") + 2 * MERGES * i + d + 1)
                            nc.vector.tensor_tensor(heads(g_t[d]), bc_mid(ident, 4), heads(ps(6 + d)), ALU.subtract)
                            nc.vector.tensor_tensor(heads(g_u[d]), bc_mid(ident, 4), heads(g_am[d]), ALU.subtract).then_inc(sem("gd_tu"), 1)
                        else:
                            dve.wait_ge(sem("gd_y"), before(L, "gd_y") + 2 * ((MERGES - 1) * i + m - 1) + d + 1)
                            nc.vector.tensor_tensor(g_t[d], g_t[d], ps(4 + d), ALU.subtract)
                            nc.vector.tensor_tensor(g_u[d], g_u[d], ps(2 + d), ALU.subtract).then_inc(sem("gd_tu"), 1)
                for d in range(2):
                    dve.wait_ge(sem("gd_y"), before(L, "gd_y") + 2 * ((MERGES - 1) * i + MERGES - 2) + d + 1)
                    nc.vector.tensor_tensor(g_u[d], g_u[d], ps(2 + d), ALU.subtract).then_inc(sem("gd_solved"), 1)
                for d in range(2):
                    dve.wait_ge(sem("gd_uw"), before(L, "gd_uw") + 2 * i + d + 1)
                    src, dst = heads(ps(6 + d)), heads(g_x[d])
                    nc.vector.tensor_tensor(dst[:, :, 0:HD], src[:, :, 0:HD], bc_in(g_beta[:, i, 4 * d:4 * d + 4], HD), ALU.mult)
                    nc.vector.tensor_tensor(dst[:, :, HD:P], src[:, :, HD:P], bc_in(g_nbeta[:, i, 4 * d:4 * d + 4], HD), ALU.mult).then_inc(sem("gd_uws"), 1)
                for d in range(2):
                    finish(i, d)
            dve.wait_ge(sem("gd_evac_act"), before(L, "gd_evac_act") + 2 * NT)
            for step in range(1, NT):
                for d in range(2):
                    a, b = ORDERS[d][step - 1], ORDERS[d][step]
                    if step == 1:
                        ins = nc.vector.tensor_copy(SST[:, b, d, :], DS[:, a, d, :])
                    else:
                        dve.wait_ge(sem("gd_scan_mm"), before(L, "gd_scan_mm") + 2 * (step - 2) + d + 1)
                        ins = nc.vector.tensor_tensor(SST[:, b, d, :], DS[:, a, d, :], ps(2 + d, P), ALU.add)
                    ins.then_inc(sem("gd_scan"), 1)
            dve.wait_ge(sem("gd_scan"), before(L, "gd_scan") + 2 * (NT - 1))
            nc.vector.memset(stat[:, 63:64], 0.0).then_inc(sem("scanned"), 1)

        def gd_gates_act(act, L):
            nc.scalar.activation(nea, alog[:, L, :], ACT.Exp).then_inc(sem("gd_nea_exp"), 1)
            act.wait_ge(sem("proj_evac"), plan.proj_no[L, "gd", 0, NT - 1] + 1)
            nc.scalar.activation(g_beta, P4[:, :, 8:16], ACT.Sigmoid)
            act.wait_ge(sem("gd_abs"), before(L, "gd_abs") + 1)
            achain(nc.scalar.activation(g_t2, g_t2, ACT.Exp, scale=-1.0))
            nc.scalar.activation(g_t2, g_t2, ACT.Ln, bias=ones[:, 0:1]).then_inc(sem("gd_sp"), 1)

        def gd_conv_act(act, L, f):
            act.wait_ge(sem("gd_cv"), before(L, "gd_cv") + f + 1)
            if f >= 2:
                act.wait_ge(sem("gd_silu"), before(L, "gd_silu") + f - 1)
            nc.scalar.activation(g_ev[f % 2], g_cv[f % 2], ACT.Sigmoid).then_inc(sem("gd_cve"), 1)

        def gd_act(act, L):
            act.wait_ge(sem("gd_sums"), before(L, "gd_sums") + 1)
            nc.scalar.activation(g_eg, ps(7, 144), ACT.Exp).then_inc(sem("gd_cum"), 1)
            for i in range(NT):
                act.wait_ge(sem("gd_turn"), before(L, "gd_turn") + i + 1)
                if i == 0:
                    act.wait_ge(sem("gd_silu"), before(L, "gd_silu") + 6)
                else:
                    act.wait_ge(sem("gd_tiled"), before(L, "gd_tiled") + i)
                nc.scalar.activation(g_x[0], ps(2), ACT.Square)
                nc.scalar.activation(g_v, ps(3, 256), ACT.Copy).then_inc(sem("gd_sq"), 1)
                act.wait_ge(sem("gd_ss"), before(L, "gd_ss") + i + 1)
                achain(nc.scalar.activation(small[:, 8:16], small[:, 0:8], ACT.Ln, bias=eps_col))
                if i >= 1:
                    act.wait_ge(sem("gd_qkn"), before(L, "gd_qkn") + i)
                nc.scalar.activation(small[:, 16:24], small[:, 8:16], ACT.Exp, scale=-0.5).then_inc(sem("gd_rs"), 1)
                for d in range(2):
                    act.wait_ge(sem("gd_gam"), before(L, "gd_gam") + 2 * i + d + 1)
                    nc.scalar.activation(g_gm[d], ps(6 + d), ACT.Exp).then_inc(sem("gd_gm"), 1)
                act.wait_ge(sem("gd_turn2"), before(L, "gd_turn2") + i + 1)
                nc.scalar.activation(g_qkT, ps(2), ACT.Copy).then_inc(sem("gd_turn2_evac"), 1)
                if L + 1 < DEPTH:
                    mod_evac(act, L + 1, 2 * i)
                for m in range(1, MERGES):
                    for d in range(2):
                        act.wait_ge(sem("gd_x"), before(L, "gd_x") + 2 * (MERGES * i + m) + d + 1)
                        nc.scalar.activation(g_x[d], ps(6 + d), ACT.Copy).then_inc(sem("gd_xe"), 1)
                if L + 1 < DEPTH:
                    mod_evac(act, L + 1, 2 * i + 1)
                for d in range(2):
                    act.wait_ge(sem("gd_fin"), before(L, "gd_fin") + 2 * i + d + 1)
                    nc.scalar.activation(QX_of["gd"][:, i, d, :], ps(2 + d, 256), ACT.Copy)
                    act.wait_ge(sem("gd_evac_dve"), before(L, "gd_evac_dve") + 2 * i + d + 1)
                    nc.scalar.activation(DS[:, i, d, :], psum[:, 4 + d, 256:384], ACT.Copy).then_inc(sem("gd_evac_act"), 1)
            if L + 1 < DEPTH:
                mod_keep(act, L + 1)

        def gd_pe(pe, L):
            pe.wait_ge(sem("gd_conv"), before(L, "gd_conv") + 1)
            for i in range(NT):
                if i >= 1:
                    pe.wait_ge(sem("gd_evac_act"), before(L, "gd_evac_act") + 2 * i)
                for b in range(6):
                    ins = nc.tensor.transpose(psum[:, 2 + b // 4, P * (b % 4):P * (b % 4) + P], FM[:, b, tile_cols(i)], ident)
                ins.then_inc(sem("gd_turn"), 1)
                if i == 0:
                    pe.wait_ge(sem("gd_gate"), before(L, "gd_gate") + 1)
                    for d in range(2):
                        g = g_gate[:, :, 4 * d:4 * d + 4]
                        nc.tensor.matmul(psum[:, 7, 24 * d:24 * d + 24].rearrange("p (t h) -> p t h", t=NT), run[d], g, start=True, stop=True)
                        nc.tensor.matmul(psum[:, 7, 48 + 24 * d:72 + 24 * d].rearrange("p (t h) -> p t h", t=NT), tail[d], g, start=True, stop=True)
                    nc.tensor.matmul(psum[:, 7, 96:144].rearrange("p (t h) -> p t h", t=NT), ones, g_gate, start=True, stop=True).then_inc(sem("gd_sums"), 1)
                for d in range(2):
                    pe.wait_ge(sem("gd_ga"), before(L, "gd_ga") + 2 * i + d + 1)
                    if d == 1 and i == 0:
                        pe.wait_ge(sem("gd_cum"), before(L, "gd_cum") + 1)
                    nc.tensor.matmul(ps(6 + d), tail[d], g_gm[d], start=True, stop=True).then_inc(sem("gd_gam"), 1)
                pe.wait_ge(sem("gd_qkn"), before(L, "gd_qkn") + i + 1)
                for b in range(4):
                    ins = nc.tensor.transpose(psum[:, 2, P * b:P * b + P], g_qkn[:, P * b:P * b + P], ident)
                ins.then_inc(sem("gd_turn2"), 1)
                pe.wait_ge(sem("gd_turn2_evac"), before(L, "gd_turn2_evac") + i + 1)
                for h in range(HEADS):
                    q = g_qkT[half_of(h), P * (h // 2):P * (h // 2) + P]
                    k = g_qkT[half_of(h), 256 + P * (h // 2):256 + P * (h // 2) + P]
                    nc.tensor.matmul(psum[:, 4 + h % 2, P * (h // 2):P * (h // 2) + P], k, q, start=True, stop=True)
                    ins = nc.tensor.matmul(psum[:, 4 + h % 2, 256 + P * (h // 2):256 + P * (h // 2) + P], k, k, start=True, stop=True)
                ins.then_inc(sem("gd_scores"), 1)
                if L + 1 < DEPTH:
                    mod_mm(pe, L + 1, 2 * i)
                for m in range(MERGES):
                    for d in range(2):
                        pe.wait_ge(sem("gd_am"), before(L, "gd_am") + 2 * (MERGES * i + m) + d + 1)
                        if m >= 1:
                            pe.wait_ge(sem("gd_tu"), before(L, "gd_tu") + 2 * ((MERGES - 1) * i + m - 1) + d + 1)
                        for h in range(HEADS):
                            c = slice(P * h, P * h + P)
                            ins = nc.tensor.matmul(psum[:, 6 + d, c], g_am[d][:, c], g_t[d][:, c] if m else ident, start=True, stop=True)
                        ins.then_inc(sem("gd_x"), 1)
                    if m == 0:
                        continue
                    for d in range(2):
                        pe.wait_ge(sem("gd_xe"), before(L, "gd_xe") + 2 * ((MERGES - 1) * i + m - 1) + d + 1)
                        if m == 1:
                            pe.wait_ge(sem("gd_at"), before(L, "gd_at") + 2 * i + 2)
                        for h in range(HEADS):
                            c = slice(P * h, P * h + P)
                            if m < MERGES - 1:
                                nc.tensor.matmul(psum[:, 4 + d, c], g_u[d][:, c], g_x[d][:, c], start=True, stop=True)
                            ins = nc.tensor.matmul(psum[:, 2 + d, c], g_x[d][:, c], g_u[d][:, c], start=True, stop=True)
                        ins.then_inc(sem("gd_y"), 1)
                if L + 1 < DEPTH:
                    mod_turn(pe, L + 1, 2 * i)
                    mod_mm(pe, L + 1, 2 * i + 1)
                for d in range(2):
                    pe.wait_ge(sem("gd_solved"), before(L, "gd_solved") + 2 * i + d + 1)
                    pe.wait_ge(sem("gd_tiled"), before(L, "gd_tiled") + i + 1)
                    for h in range(HEADS):
                        ins = nc.tensor.matmul(psum[:, 6 + d, P * h:P * h + P], g_u[d][:, P * hpos(h):P * hpos(h) + P],
                                               g_r[:, d, P * h:P * h + P], start=True, stop=True)
                    ins.then_inc(sem("gd_uw"), 1)
                for d in range(2):
                    pe.wait_ge(sem("gd_uws"), before(L, "gd_uws") + 2 * i + d + 1)
                    pe.wait_ge(sem("gd_pmm"), before(L, "gd_pmm") + 2 * i + d + 1)
                    for pair in range(2):
                        c = slice(P * pair, P * pair + P)
                        nc.tensor.matmul(psum[:, 2 + d, c], g_qt[:, d, c], ident, start=True, stop=False, skip_group_check=True)
                        for h in (2 * pair, 2 * pair + 1):
                            nc.tensor.matmul(psum[half_of(h), 2 + d, c], g_x[d][:, P * h + HD:P * h + P],
                                             g_pm[d][:, P * hpos(h):P * hpos(h) + P], start=False, stop=True, skip_group_check=True)
                    for h in range(HEADS):
                        u, w = g_x[d][:, P * h:P * h + HD], g_x[d][:, P * h + HD:P * h + P]
                        kt = g_kt[:, d, HD * h:HD * h + HD]
                        nc.tensor.matmul(psum[:, 4 + d, HD * h:HD * h + HD], g_pm[d][:, P * hpos(h):P * hpos(h) + P], u, start=True, stop=True)
                        o = HD * (h // 2)
                        nc.tensor.matmul(psum[half_of(h), 4 + d, 256 + o:320 + o], kt, u, start=True, stop=True)
                        ins = nc.tensor.matmul(psum[half_of(h), 4 + d, 384 + o:448 + o], w, kt, start=True, stop=True)
                    ins.then_inc(sem("gd_fin"), 1)
                if L + 1 < DEPTH:
                    mod_turn(pe, L + 1, 2 * i + 1)
            for step in range(2, NT):
                for d in range(2):
                    a = ORDERS[d][step - 1]
                    pe.wait_ge(sem("gd_scan"), before(L, "gd_scan") + 2 * (step - 2) + d + 1)
                    if step == 2:
                        pe.wait_ge(sem("gd_evac_dve"), before(L, "gd_evac_dve") + 2 * NT)
                    for h in range(HEADS):
                        rows, c = half_of(h), slice(HD * (h // 2), HD * (h // 2) + HD)
                        ins = nc.tensor.matmul(psum[rows, 2 + d, c], MT[rows, a, d, c], SST[rows, a, d, c], start=True, stop=True)
                    ins.then_inc(sem("gd_scan_mm"), 1)

        DG = [regB[:, 4096 + 512 * b:4608 + 512 * b] for b in range(2)]
        ME = [regB[:, 5120 + 512 * b:5632 + 512 * b] for b in range(2)]
        MP = [regB[:, 6144 + 512 * b:6656 + 512 * b] for b in range(2)]
        hT2, mT = hT, yT
        ROWS = [(w, s, jj) for w in range(2) for s in range(2) for jj in range(2)]

        def merge_keys(L):
            return [(n, half, i) for n in range(4) for half in range(2) for i in out_tiles(L)]

        def merge_pool(pool, L):
            pool.wait_ge(sem("yT"), ended("yT", L, "gd") + 1)
            pool.dma_start(wrt[:, :, :], A["w_router"][L].rearrange("(k p) e -> p k e", p=P)).then_inc(sem("router_loaded"), 16)
            for i in out_tiles(L):
                pool.dma_start(XF(i), x_in(L, i)).then_inc(sem("xf_loaded"), 16)
            for q, (w, s, jj) in enumerate(ROWS):
                if q >= 2:
                    pool.wait_ge(sem("row_mm"), before(L, "row_mm") + q - 1)
                v = modv[:, 16 + 24 * w + 4 * jj:20 + 24 * w + 4 * jj, s]
                nc.gpsimd.tensor_tensor(heads(DG[q % 2]), bc_mid(ident, 4), bc_in(v, P), ALU.mult).then_inc(sem("row_diag"), 1)
            nt = len(out_tiles(L))
            for r, (n, half, i) in enumerate(merge_keys(L)):
                if n == 0:
                    continue
                pool.wait_ge(sem("merge_prod"), merge_before(L) + r + 1)
                cols = M[:, i, SLOTW * half:SLOTW * half + SLOTW]
                nc.gpsimd.tensor_tensor(cols, cols, MP[r % 2], ALU.add).then_inc(sem("merge_sum"), 1)
            for q, i in enumerate(out_tiles(L)):
                pool.wait_ge(sem("xg_done"), mid_before(L) + q + 1)
                pool.dma_start(xn_ffn[L][tok_tile(q), :], XN(i)).then_inc(sem("mid_stored"), 16)

        def merge_before(L):
            return L * len(merge_keys(0))

        def mid_before(L):
            return L * NT

        def merge_act(act, L):
            for q, (w, s, jj) in enumerate(ROWS):
                act.wait_ge(sem("row_mm"), before(L, "row_mm") + q + 1)
                nc.scalar.activation(GROW[:, w, s, 512 * jj:512 * jj + 512], ps(4 + q % 2), ACT.Copy).then_inc(sem("row_evac"), 1)
            for r, (n, half, i) in enumerate(merge_keys(L)):
                act.wait_ge(sem("jobs_done"), plan.job_no[L, "merge", n, half, i])
                if r >= 2:
                    act.wait_ge(sem("merge_prod"), merge_before(L) + r - 1)
                nc.scalar.activation(ME[r % 2], ps(r % 2), ACT.Sigmoid).then_inc(sem("merge_gate"), 1)
            for q, i in enumerate(out_tiles(L)):
                act.wait_ge(sem("m_turn"), mid_before(L) + q + 1)
                for b in range(2):
                    ins = nc.scalar.activation(mT[:, 4 * b:4 * b + 4, tok_tile(i)], heads(ps(4 + b)), ACT.Copy)
                ins.then_inc(sem("m_turn_evac"), 1)
            for q, i in enumerate(out_tiles(L)):
                b = 2 * (q % 2)
                act.wait_ge(sem("jobs_done"), plan.job_no[L, "out", i, 1])
                st = stat[:, 0:16].rearrange("p (b c) -> p b c", b=2)[:, q % 2, :]
                if q >= 2:
                    act.wait_ge(sem("mid_done"), mid_before(L) + q - 1)
                junk = ME[q % 2]
                for hb in range(2):
                    achain(nc.scalar.activation(junk, ps(b + hb), ACT.Square, accum_out=st[:, hb:hb + 1]))
                achain(nc.scalar.activation(st[:, 2:3], st[:, 0:1], ACT.Identity, bias=st[:, 1:2]))
                achain(nc.scalar.activation(st[:, 3:4], st[:, 2:3], ACT.Ln, bias=eps_col, scale=1.0 / D))
                nc.scalar.activation(st[:, 4:5], st[:, 3:4], ACT.Exp, scale=-0.5).then_inc(sem("mid_rstd"), 1)
                act.wait_ge(sem("mid_done"), mid_before(L) + q + 1)
                achain(nc.scalar.activation(XN(i), XF(i), ACT.Square, accum_out=st[:, 5:6]))
                achain(nc.scalar.activation(st[:, 6:7], st[:, 5:6], ACT.Ln, bias=eps_col, scale=1.0 / D))
                achain(nc.scalar.activation(st[:, 7:8], st[:, 6:7], ACT.Exp, scale=-0.5))
                nc.scalar.activation(XN(i), XF(i), ACT.Copy, scale=st[:, 7:8]).then_inc(sem("xg_done"), 1)

        def merge_dve(dve, L):
            for r, (n, half, i) in enumerate(merge_keys(L)):
                dve.wait_ge(sem("merge_gate"), merge_before(L) + r + 1)
                dve.wait_ge(sem("jobs_done"), plan.job_no[L, "branch", n, half, i])
                dst = M[:, i, SLOTW * half:SLOTW * half + SLOTW] if n == 0 else MP[r % 2]
                nt2 = 2 * len(out_tiles(L))
                if n and r - 2 >= nt2:
                    dve.wait_ge(sem("merge_sum"), before(L, "merge_sum") + r - 2 - nt2 + 1)
                nc.vector.tensor_tensor(dst, ME[r % 2], ps(2 + r % 2), ALU.mult).then_inc(sem("merge_prod"), 1)
            for q, i in enumerate(out_tiles(L)):
                s, b = (0 if i < CT else 1), 2 * (q % 2)
                dve.wait_ge(sem("mid_rstd"), mid_before(L) + q + 1)
                if q == 0:
                    dve.wait_ge(sem("xf_loaded"), 16 * (mid_before(L) + len(out_tiles(L))))
                    dve.wait_ge(sem("row_evac"), before(L, "row_evac") + 8)
                rstd = stat[:, 8 * (q % 2) + 4:8 * (q % 2) + 5]
                t = regB[:, 6144:7168].rearrange("p (b c) -> p b c", b=2)
                dchain(nc.vector.scalar_tensor_tensor(out=t, in0=psum[:, b:b + 2, :], scalar=rstd,
                                                      in1=GROW[:, 0, s, :].rearrange("p (b c) -> p b c", b=2), op0=ALU.mult, op1=ALU.mult))
                x = XF(i)
                nc.vector.tensor_tensor(x, x, regB[:, 6144:7168], ALU.add).then_inc(sem("mid_done"), 1)
                if q >= 1:
                    ffn_modulate(dve, L, q - 1)
            ffn_modulate(dve, L, len(out_tiles(L)) - 1)

        def ffn_modulate(dve, L, q):
            i = out_tiles(L)[q]
            s = 0 if i < CT else 1
            dve.wait_ge(sem("g_turned"), mid_before(L) + q + 1)
            for k in range(KB):
                ins = nc.vector.tensor_scalar(hT2[:, k, tok_tile(i)], psum[:, 6 + k // 4, P * (k % 4):P * (k % 4) + P],
                                              modv[:, 32 + k, s:s + 1], modv[:, 24 + k, s:s + 1], ALU.mult, ALU.add)
            ins.then_inc(sem("g_evac"), 1)

        def merge_pe(pe, L):
            pe.wait_ge(sem("yT"), ended("yT", L, "gd") + 1)
            for q in range(8):
                pe.wait_ge(sem("row_diag"), before(L, "row_diag") + q + 1)
                if q >= 2:
                    pe.wait_ge(sem("row_evac"), before(L, "row_evac") + q - 1)
                nc.tensor.matmul(ps(4 + q % 2), ones, DG[q % 2], start=True, stop=True).then_inc(sem("row_mm"), 1)
            if L + 1 < DEPTH:
                pe.wait_ge(sem("mod_raw"), L + 2)
            for r, (n, half, i) in enumerate(merge_keys(L)):
                wm = wait_item(pe, L, "merge", n, half)
                pe.wait_ge(sem(f"branch{half}_loaded"), 16 * (4 * L + n + 1))
                wb = w_branch(half)
                if r >= 2:
                    pe.wait_ge(sem("merge_prod"), merge_before(L) + r - 1)
                for k in range(KB):
                    ins = nc.tensor.matmul(ps(r % 2), hT[:, k, tok_tile(i)], wm[:, k, :], start=(k == 0), stop=(k == KB - 1))
                ins.then_inc(sem("jobs_done"), 1)
                for k in range(2):
                    ins = nc.tensor.matmul(ps(2 + r % 2), yT[:, 2 * n + k, tok_tile(i)], wb[:, k, :], start=(k == 0), stop=(k == 1))
                ins.then_inc(sem("jobs_done"), 1)
            pe.wait_ge(sem("merge_sum"), before(L, "merge_sum") + 6 * len(out_tiles(L)))
            pe.wait_ge(sem("row_evac"), before(L, "row_evac") + 8)
            for q, i in enumerate(out_tiles(L)):
                if q >= 1:
                    pe.wait_ge(sem("m_turn_evac"), mid_before(L) + q)
                for k in range(KB):
                    ins = nc.tensor.transpose(psum[:, 4 + k // 4, P * (k % 4):P * (k % 4) + P], M[:, i, P * k:P * k + P], ident)
                ins.then_inc(sem("m_turn"), 1)
            pe.wait_ge(sem("merge_prod"), merge_before(L) + len(merge_keys(L)))
            wt = [wait_item(pe, L, "out", half) for half in range(2)]

            def turn(q):
                i = out_tiles(L)[q]
                pe.wait_ge(sem("xg_done"), mid_before(L) + q + 1)
                if q >= 1:
                    pe.wait_ge(sem("g_evac"), mid_before(L) + q)
                for k in range(KB):
                    ins = nc.tensor.transpose(psum[:, 6 + k // 4, P * (k % 4):P * (k % 4) + P], XN(i)[:, P * k:P * k + P], ident)
                ins.then_inc(sem("g_turned"), 1)

            for q, i in enumerate(out_tiles(L)):
                b = 2 * (q % 2)
                pe.wait_ge(sem("m_turn_evac"), mid_before(L) + q + 1)
                if q >= 2:
                    pe.wait_ge(sem("mid_done"), mid_before(L) + q - 1)
                for half in range(2):
                    for k in range(KB):
                        ins = nc.tensor.matmul(ps(b + half), mT[:, k, tok_tile(i)], wt[half][:, k, :], start=(k == 0), stop=(k == KB - 1))
                    ins.then_inc(sem("jobs_done"), 1)
                if q >= 1:
                    turn(q - 1)
            turn(len(out_tiles(L)) - 1)

        AFF = T[:, 0:96].rearrange("p (t e) -> p t e", t=NT)
        AFT = T[0:EXPERTS, 128:128 + TOK]
        VAL = T[0:EXPERTS, 1024:1024 + 96]
        IDX = T[0:EXPERTS, 1152:1152 + 96].bitcast(U32)
        IDXF = T[0:EXPERTS, 1280:1280 + 96]
        VALT = T[0:96, 1408:1408 + EXPERTS]
        IDXT = T[0:96, 1440:1440 + EXPERTS + 1].bitcast(U32)
        IDXS = [T[0:96, 1472 + 2 * b:1473 + 2 * b].bitcast(U32) for b in range(2)]
        VCUR = T[0:96, 1480:1481]
        XE = regA[0:96, 1536:2560]
        XET = regA[:, 2560:3328].rearrange("p (k c) -> p k c", k=KB)
        SG = [regA[:, 3328 + 512 * b:3840 + 512 * b] for b in range(2)]
        HACT = regA[:, 4352:5376]
        HAT = regA[:, 5376:6144].rearrange("p (k c) -> p k c", k=KB)
        YE = regA[0:96, 6144:7168]
        mxr, smr = regB[:, 7168:7184], regB[:, 7184:7200]
        ZERO = regB[:, 4096:5120]

        def caps(L):
            lat = (CTX, SEQ, 0, CAP_LAT)
            return [lat, (0, CTX, CAP_LAT, CAP_CTX)] if L < DEPTH - 1 else [lat]

        def ncol(L):
            return CAP_LAT + (CAP_CTX if L < DEPTH - 1 else 0)

        LAT_W, CTX_W = SLOTW * CAP_LAT // P, SLOTW * CAP_CTX // P

        def hidden_width(L):
            return LAT_W + (CTX_W if len(caps(L)) > 1 else 0)

        def moe_pe(pe, L):
            tiles = out_tiles(L)
            pe.wait_ge(sem("g_evac"), mid_before(L) + len(tiles))
            pe.wait_ge(sem("router_loaded"), 16 * (L + 1))
            for q, i in enumerate(tiles):
                for k in range(KB):
                    ins = nc.tensor.matmul(psum[:, 4, EXPERTS * q:EXPERTS * q + EXPERTS], hT2[:, k, tok_tile(i)], wrt[:, k, :], start=(k == 0), stop=(k == KB - 1))
            ins.then_inc(sem("router_pe"), 1)
            pe.wait_ge(sem("router_dve"), 4 * L + 2)
            for q, i in enumerate(tiles):
                o = P * i
                ins = nc.tensor.transpose(psum[0:EXPERTS, 6 + o // 512, o % 512:o % 512 + P], AFF[:, q, :], ident)
            ins.then_inc(sem("router_pe"), 1)
            n, wc = ncol(L), hidden_width(L)
            pe.wait_ge(sem("router_dve"), 4 * L + 3)
            nc.tensor.transpose(psum[0:n, 4, 0:EXPERTS], VAL[:, 0:n], ident[0:EXPERTS, 0:EXPERTS])
            nc.tensor.transpose(psum[0:n, 4, 32:32 + EXPERTS], IDXF[:, 0:n], ident[0:EXPERTS, 0:EXPERTS]).then_inc(sem("router_pe"), 1)

            def flip(k, dst, src):
                m = src.shape[0]
                if k == 0:
                    return nc.tensor.matmul(dst, src, ident[0:m, 0:m], start=True, stop=True)
                return nc.tensor.transpose(dst, src, ident[0:m, 0:m])

            def turn_x(gathered):
                pe.wait_ge(sem("gathered"), gathered)
                for k in range(KB):
                    ins = flip(k, psum[:, 4 + k // 4, n * (k % 4):n * (k % 4) + n], XE[0:n, P * k:P * k + P])
                ins.then_inc(sem("x_turned"), 1)

            pe.wait_ge(sem("router_dve"), 4 * L + 4)
            turn_x(16 * ((EXPERTS + 1) * L + 1))
            item0, first = plan.item_no[L, "moe", 0, 0], plan.job_no[L, "moe", 0, 0]
            with pe.Fori(0, EXPERTS) as e:
                pe.wait_ge(sem("xeT_ready"), e + ((EXPERTS + 1) * L + 1))

                def item(j):
                    m = item0 + j
                    pe.wait_ge(sem(f"slot{slot_of(m)}_loaded"), e * 32 + loaded_value(m))
                    return ring[:, slot_of(m)]

                for j in range(4):
                    w = item(j)
                    if j == 0:
                        pe.wait_ge(sem("ye_done"), e + ((EXPERTS + 1) * L + 1))
                    for k in range(KB):
                        for g in range(P // CAP_LAT):
                            ins = nc.tensor.matmul(psum[CAP_LAT * g:CAP_LAT * g + CAP_LAT, j, 0:LAT_W], XET[:, k, 0:CAP_LAT],
                                                   w[:, k, LAT_W * g:LAT_W * g + LAT_W], start=(k == 0), stop=(k == KB - 1))
                    for k in range(KB):
                        for g in range(P // CAP_CTX if wc > LAT_W else 0):
                            ins = nc.tensor.matmul(psum[CAP_CTX * g:CAP_CTX * g + CAP_CTX, j, LAT_W:wc], XET[:, k, CAP_LAT:n],
                                                   w[:, k, CTX_W * g:CTX_W * g + CTX_W], start=(k == 0), stop=(k == KB - 1))
                    ins.then_inc(sem("jobs_done"), 1)
                turn_x(e * 16 + 16 * ((EXPERTS + 1) * L + 2))
                for half in range(2):
                    pe.wait_ge(sem("hidden"), 2 * e + (2 * EXPERTS * L + half + 1))
                    for k in range(wc // P):
                        ins = flip(k, psum[:, 6 + half, P * k:P * k + P], HACT[:, 512 * half + P * k:512 * half + P * k + P])
                    ins.then_inc(sem("hidden_turned"), 1)
                for half in range(2):
                    w = item(4 + half)
                    if half == 0:
                        pe.wait_ge(sem("hidden_T"), 2 * e + (2 * EXPERTS * L + 2))
                    for k in range(KB):
                        ins = nc.tensor.matmul(psum[0:n, half, :], HAT[:, k, 0:n], w[:, k, :], start=(k == 0), stop=(k == KB - 1))
                    ins.then_inc(sem("jobs_done"), 1)

        def moe_dve(dve, L):
            tiles = out_tiles(L)
            nt, n, wc = len(tiles), ncol(L), hidden_width(L)
            dve.wait_ge(sem("router_pe"), 3 * L + 1)
            lg = ps(4, EXPERTS * nt).rearrange("p (t e) -> p t e", t=nt)
            dchain(nc.vector.tensor_reduce(mxr[:, 0:nt], lg, AX.X, ALU.max))
            nc.vector.tensor_tensor(AFF[:, 0:nt, :], lg, bc_in(mxr[:, 0:nt], EXPERTS), ALU.subtract).then_inc(sem("router_dve"), 1)
            dve.wait_ge(sem("aff_exp"), L + 1)
            dchain(nc.vector.tensor_reduce(smr[:, 0:nt], AFF[:, 0:nt, :], AX.X, ALU.add))
            dchain(nc.vector.reciprocal(smr[:, 0:nt], smr[:, 0:nt]))
            nc.vector.tensor_tensor(AFF[:, 0:nt, :], AFF[:, 0:nt, :], bc_in(smr[:, 0:nt], EXPERTS), ALU.mult).then_inc(sem("router_dve"), 1)
            dve.wait_ge(sem("router_pe"), 3 * L + 2)
            lo = P * tiles[0]
            dchain(nc.vector.tensor_copy(AFT[:, lo:TOK], psum[0:EXPERTS, 6:8, :].rearrange("p b c -> p (b c)")[:, lo:TOK]))
            for t0, tn, c0, cn in caps(L):
                a = AFT[:, t0:t0 + tn]
                for r in range(cn // 8):
                    v = VAL[:, c0 + 8 * r:c0 + 8 * r + 8]
                    dchain(nc.vector.max(v, a))
                    dchain(nc.vector.max_index(IDX[:, c0 + 8 * r:c0 + 8 * r + 8], v, a))
                    if r < cn // 8 - 1:
                        dchain(nc.vector.match_replace(a, v, a, -1.0))
            dchain(nc.vector.tensor_copy(IDXF[:, 0:n], IDX[:, 0:n]))
            nc.vector.tensor_scalar(IDXF[:, 0:CAP_LAT], IDXF[:, 0:CAP_LAT], float(CTX - P * tiles[0]), None, ALU.add).then_inc(sem("router_dve"), 1)
            dve.wait_ge(sem("router_pe"), 3 * L + 3)
            nc.vector.tensor_copy(VALT[0:n, :], psum[0:n, 4, 0:EXPERTS])
            nc.vector.tensor_copy(IDXT[0:n, 0:EXPERTS], psum[0:n, 4, 32:32 + EXPERTS])
            nc.vector.tensor_copy(IDXT[0:n, EXPERTS:EXPERTS + 1], psum[0:n, 4, 32:33]).then_inc(sem("router_dve"), 1)

            def scale_x():
                for s, (t0, tn, c0, cn) in ((1, caps(L)[0]),) + (((0, caps(L)[1]),) if len(caps(L)) > 1 else ()):
                    for b in range(2):
                        src = psum[:, 4 + b, 0:4 * n].rearrange("p (k c) -> p k c", k=4)[:, :, c0:c0 + cn]
                        dst = XET[:, 4 * b:4 * b + 4, c0:c0 + cn]
                        nc.vector.tensor_tensor(dst, src, bc_in(modv[:, 32 + 4 * b:36 + 4 * b, s], cn), ALU.mult)
                nc.vector.memset(stat[:, 58:59], 0.0).then_inc(sem("xeT_scaled"), 1)

            dve.wait_ge(sem("x_turned"), (EXPERTS + 1) * L + 1)
            scale_x()
            with dve.Fori(0, EXPERTS) as e:
                for half in range(2):
                    dve.wait_ge(sem("silu_gate"), 2 * e + (2 * EXPERTS * L + half + 1))
                    sg = SG[half][:, 0:wc]
                    nc.vector.tensor_tensor(sg, sg, psum[:, 2 * half, 0:wc], ALU.mult).then_inc(sem("gate_prod"), 1)
                    dve.wait_ge(sem("gate_prod"), 2 * e + (2 * EXPERTS * L + half + 1))
                    dve.wait_ge(sem("jobs_done"), 6 * e + (plan.job_no[L, "moe", 0, 0] + 2 * half + 1))
                    nc.vector.tensor_tensor(HACT[:, 512 * half:512 * half + wc], sg, psum[:, 2 * half + 1, 0:wc], ALU.mult).then_inc(sem("hidden"), 1)
                dve.wait_ge(sem("x_turned"), e + ((EXPERTS + 1) * L + 2))
                scale_x()
                dve.wait_ge(sem("hidden_turned"), 2 * e + (2 * EXPERTS * L + 2))
                for half in range(2):
                    hat, flipped = HAT[:, 4 * half:4 * half + 4, :], psum[:, 6 + half, 0:wc]
                    if wc > LAT_W:
                        nc.vector.tensor_copy(hat[:, :, CAP_LAT:n], flipped[:, LAT_W:wc].rearrange("p (g c) -> p g c", g=4))
                    nc.vector.tensor_copy(hat[:, :, 0:CAP_LAT].rearrange("p (g b) c -> p g b c", g=2),
                                          flipped[:, 0:LAT_W].rearrange("p (b g c) -> p g b c", b=2, g=2)).then_inc(sem("hidden_T"), 1)

        def moe_act(act, L):
            nt, n, wc = len(out_tiles(L)), ncol(L), hidden_width(L)
            act.wait_ge(sem("router_dve"), 4 * L + 1)
            nc.scalar.activation(AFF[:, 0:nt, :], AFF[:, 0:nt, :], ACT.Exp).then_inc(sem("aff_exp"), 1)
            first = plan.job_no[L, "moe", 0, 0]
            nc.scalar.activation(stat[:, 57:58], eps_col, ACT.Copy).then_inc(sem("ye_done"), 1)
            with act.Fori(0, EXPERTS) as e:
                for half in range(2):
                    act.wait_ge(sem("jobs_done"), 6 * e + (first + 2 * half))
                    nc.scalar.activation(SG[half][:, 0:wc], psum[:, 2 * half, 0:wc], ACT.Sigmoid).then_inc(sem("silu_gate"), 1)
                act.wait_ge(sem("picked"), 2 * e + (2 * EXPERTS * L + 1))
                for half in range(2):
                    act.wait_ge(sem("jobs_done"), 6 * e + (first + 4 + half))
                    ins = nc.scalar.activation(YE[0:n, 512 * half:512 * half + 512], psum[0:n, half, :], ACT.Copy, scale=VCUR[0:n, :])
                ins.then_inc(sem("ye_done"), 1)

        def moe_pool(pool, L):
            n = ncol(L)
            pool.wait_ge(sem("row_evac"), before(L, "row_evac") + 8)
            pchain(nc.gpsimd.memset(ZERO, 0.0))
            for q in range(len(out_tiles(L))):
                pool.dma_start(ffn[L][tok_tile(q), :], ZERO).then_inc(sem("mid_stored"), 16)
            pool.wait_ge(sem("router_dve"), 4 * L + 4)
            pool.wait_ge(sem("mid_stored"), 32 * (mid_before(L) + len(out_tiles(L))))

            def gather():
                pool.indirect_dma_start(out=XE[0:n, :], out_offset=None, in_=xn_ffn[L], in_offset=bass.IndirectOffsetOnAxis(ap=IDXS[0][0:n, :], axis=0)).then_inc(sem("gathered"), 16)

            def past_wait(c):
                nc.gpsimd.tensor_tensor(stat[:, c:c + 1], eps_col, eps_col, ALU.add)

            pchain(nc.gpsimd.tensor_copy(IDXS[0][0:n, :], IDXT[0:n, 0:1]))
            gather()

            def shift_x():
                for s, (t0, tn, c0, cn) in ((1, caps(L)[0]),) + (((0, caps(L)[1]),) if len(caps(L)) > 1 else ()):
                    dst = XET[:, :, c0:c0 + cn]
                    ins = nc.gpsimd.tensor_tensor(dst, dst, bc_in(modv[:, 24:32, s], cn), ALU.add)
                ins.then_inc(sem("xeT_ready"), 1)

            pool.wait_ge(sem("xeT_scaled"), (EXPERTS + 1) * L + 1)
            shift_x()
            with pool.Fori(0, EXPERTS) as e:
                nc.gpsimd.tensor_copy(IDXS[1][0:n, :], IDXT[0:n, bass.ds(e, 1)])
                nc.gpsimd.tensor_copy(VCUR[0:n, :], VALT[0:n, bass.ds(e, 1)]).then_inc(sem("picked"), 1)
                pool.wait_ge(sem("x_turned"), e + ((EXPERTS + 1) * L + 1))
                nc.gpsimd.tensor_copy(IDXS[0][0:n, :], IDXT[0:n, bass.ds(e + 1, 1)]).then_inc(sem("picked"), 1)
                pool.wait_ge(sem("picked"), 2 * e + (2 * EXPERTS * L + 2))
                past_wait(55)
                gather()
                pool.wait_ge(sem("xeT_scaled"), e + ((EXPERTS + 1) * L + 2))
                shift_x()
                pool.wait_ge(sem("ye_done"), e + ((EXPERTS + 1) * L + 2))
                past_wait(56)
                pool.indirect_dma_start(out=ffn[L], out_offset=bass.IndirectOffsetOnAxis(ap=IDXS[1][0:n, :], axis=0), in_=YE[0:n, :],
                                        in_offset=None, compute_op=ALU.add).then_inc(sem("scattered"), 16)
                pool.wait_ge(sem("scattered"), e * 16 + (16 * EXPERTS * L + 16))

        def halves(L):
            tiles = out_tiles(L)
            return [(2 * q // len(tiles), q, i) for q, i in enumerate(tiles)]

        def post_pool(pool, L):
            pool.wait_ge(sem("xeT_ready"), (EXPERTS + 1) * (L + 1))
            for hf, q, i in halves(L):
                pool.dma_start(XN(i), ffn[L][tok_tile(q), :]).then_inc(sem(f"ffn_loaded{hf}"), 16)
            for hf, q, i in halves(L):
                pool.wait_ge(sem("post_done"), mid_before(L) + q + 1)
                dst = x_end[tok_tile(i), :] if L < DEPTH - 1 else out[0, tok_tile(i - CT), :]
                pool.dma_start(dst, XF(i)).then_inc(sem("end_stored"), 16)
            pool.wait_ge(sem("end_stored"), 16 * (mid_before(L) + len(out_tiles(L))))

        def post_act(act, L):
            nh = len(out_tiles(L)) // 2
            for hf in range(2):
                act.wait_ge(sem(f"ffn_loaded{hf}"), 16 * (mid_before(L) // 2 + nh))
                c = nh * hf
                for h2, q, i in halves(L):
                    if h2 == hf:
                        ins = nc.scalar.activation(regB[:, 4096 + D * (q - c):4096 + D * (q - c) + D], XN(i), ACT.Square, accum_out=stat[:, q:q + 1])
                achain(ins)
                achain(nc.scalar.activation(stat[:, 8 + c:8 + c + nh], stat[:, c:c + nh], ACT.Ln, bias=eps_col, scale=1.0 / D))
                nc.scalar.activation(stat[:, 16 + c:16 + c + nh], stat[:, 8 + c:8 + c + nh], ACT.Exp, scale=-0.5).then_inc(sem("post_rstd"), 1)

        def post_dve(dve, L):
            for hf, q, i in halves(L):
                s = 0 if i < CT else 1
                dve.wait_ge(sem("post_rstd"), 2 * L + hf + 1)
                f, x = XN(i), XF(i)
                dchain(nc.vector.scalar_tensor_tensor(out=f, in0=f, scalar=stat[:, 16 + q:17 + q],
                                                      in1=GROW[:, 1, s, :], op0=ALU.mult, op1=ALU.mult))
                nc.vector.tensor_tensor(x, x, f, ALU.add).then_inc(sem("post_done"), 1)

        def chained(engine, name):
            count = [0]

            def link(ins):
                ins.then_inc(sem(name), 1)
                count[0] += 1
                engine.wait_ge(sem(name), count[0])
            return link

        chains = {}
        dchain = lambda ins: chains["dve"](ins)
        achain = lambda ins: chains["act"](ins)
        pchain = lambda ins: chains["pool"](ins)

        block = ctx.enter_context(nc.Block())

        @block.sync
        def _(sp):
            setup_sp(sp)
            for L in range(DEPTH):
                stream_sp(sp, L)
                moe_sp(sp, L)

        @block.gpsimd
        def _(pool):
            chains["pool"] = chained(pool, "pool_chain")
            for L in range(DEPTH):
                if L == 0:
                    norm_pool(pool, L)
                ret_pool(pool, L)
                hg_pool(pool, L)
                at_pool(pool, L)
                gd_pool(pool, L)
                merge_pool(pool, L)
                moe_pool(pool, L)
                post_pool(pool, L)

        @block.scalar
        def _(act):
            chains["act"] = chained(act, "act_chain")
            setup_act(act)
            for L in range(DEPTH):
                norm_stats_act(act, L)
                if L == 0:
                    mod_act(act, L)
                norm_act(act, L)
                proj_act(act, L, "ret")
                proj_act(act, L, "hg")
                ret_act(act, L)
                end_act(act, L, "ret")
                proj_act(act, L, "at")
                hg_act(act, L)
                end_act(act, L, "hg")
                at_act(act, L)
                proj_act(act, L, "gd")
                gd_act(act, L)
                end_act(act, L, "gd")
                merge_act(act, L)
                moe_act(act, L)
                post_act(act, L)

        @block.tensor
        def _(pe):
            setup_pe(pe)
            for L in range(DEPTH):
                if L == 0:
                    mod_pe(pe, L)
                norm_pe(pe, L)
                proj_pe(pe, L, "ret")
                proj_pe(pe, L, "hg")
                ret_pe(pe, L)
                end_pe(pe, L, "ret")
                proj_pe(pe, L, "at")
                hg_pe(pe, L)
                end_pe(pe, L, "hg")
                at_pe(pe, L)
                proj_pe(pe, L, "gd")
                gd_pe(pe, L)
                end_pe(pe, L, "gd")
                merge_pe(pe, L)
                moe_pe(pe, L)

        @block.vector
        def _(dve):
            chains["dve"] = chained(dve, "dve_chain")
            setup_dve(dve)
            for L in range(DEPTH):
                norm_scale_dve(dve, L)
                if L == 0:
                    mod_dve(dve, L)
                norm_dve(dve, L)
                ret_dve(dve, L)
                scan_dve(dve, L, "ret", (sem("ret_own_evac"), before(L, "ret_own_evac") + NT))
                end_dve(dve, L, "ret")
                hg_dve(dve, L)
                scan_dve(dve, L, "hg", (sem("hg_own_evac"), before(L, "hg_own_evac") + NT))
                end_dve(dve, L, "hg")
                at_dve(dve, L)
                gd_dve(dve, L)
                end_dve(dve, L, "gd")
                merge_dve(dve, L)
                moe_dve(dve, L)
                if L + 1 < DEPTH: mod_dve(dve, L + 1)
                post_dve(dve, L)


_INS = ("x", "c", "ctx", "c_ctx", "w_ada", "b_ada", "g_pre_mix", "g_post_mix", "g_pre_ffn", "g_post_ffn",
        "w_in", "ret_norm_g", "hg_lb_logits", "hg_norm_g", "at_q_norm_g", "at_k_norm_g", "gd_conv_w",
        "gd_a_log", "gd_dt_bias", "gd_norm_g", "w_branch", "w_merge", "w_out", "w_router", "w_exp_gate",
        "w_exp_up", "w_exp_down")


def kernel(**inputs):
    import numpy as _np
    import concourse.bacc as _bacc
    from concourse import mybir as _mybir
    from concourse.bass_utils import run_bass_kernel_spmd as _run

    nc = _bacc.Bacc("TRN2", target_bir_lowering=False, num_devices=1)
    arrays = {name: _np.ascontiguousarray(inputs[name]) for name in _INS}
    arrays["tables"], arrays["merge_masks"], table_at = constants()
    aps = {name: nc.dram_tensor(name, a.shape, _mybir.dt.from_np(a.dtype), kind="ExternalInput").ap()
           for name, a in arrays.items()}
    aps["table_at"] = table_at
    out = nc.dram_tensor("out", (1, SEQ, D), _mybir.dt.float32, kind="ExternalOutput").ap()
    build(nc, aps, out)
    return _run(nc, [arrays], core_ids=[0]).results[0]["out"]
```
